# Optimizing a Trainium2 kernel written in Bass

```python
import math
import jax, jax.numpy as jnp
from jax import lax
import numpy as np

D_MODEL = 1024
BATCH = 1
SEQ = 256
DEPTH = 1

MEM_LEN = 256
EPS = 1e-6
CHUNK = 64

SSD_D_INNER = D_MODEL
SSD_HEAD_DIM = 64
SSD_HEADS = SSD_D_INNER // SSD_HEAD_DIM
SSD_GROUPS = 2
SSD_STATE = 128
SSD_CONV = 4
SSD_CONV_CH = SSD_D_INNER + 2 * SSD_GROUPS * SSD_STATE
DT_MIN = 1e-3
DT_MAX = 1e-1

GLA_HEADS = 4
GLA_DK = D_MODEL // 2
GLA_DV = D_MODEL
GLA_HEAD_K = GLA_DK // GLA_HEADS
GLA_HEAD_V = GLA_DV // GLA_HEADS
GLA_GATE_RANK = 16
GLA_TAU = 16.0

XATTN_HEADS = 4
XATTN_HEAD_DIM = D_MODEL // XATTN_HEADS

D_FF = -((-8 * D_MODEL) // (3 * 256)) * 256

IN_SIZES = (SSD_D_INNER, SSD_CONV_CH, SSD_HEADS,
            GLA_DK, GLA_DK, GLA_DV, GLA_DV, GLA_GATE_RANK,
            D_MODEL, D_MODEL)
IN_WIDTH = sum(IN_SIZES)


def rmsnorm(x, g):
    xf = x.astype(jnp.float32)
    y = xf * lax.rsqrt(jnp.mean(xf * xf, axis=-1, keepdims=True) + EPS)
    return (y * g.astype(jnp.float32)).astype(x.dtype)

def causal_dwconv(x, w, b):
    y = lax.conv_general_dilated(x, w, window_strides=(1,), padding=[(SSD_CONV - 1, 0)],
                                 dimension_numbers=('NWC', 'WIO', 'NWC'),
                                 feature_group_count=x.shape[-1])
    return y + b

def segsum_exp(a):
    L = a.shape[-1]
    cs = jnp.cumsum(a, axis=-1)
    mask = jnp.tril(jnp.ones((L, L), dtype=bool))
    diff = cs[..., :, None] - cs[..., None, :]
    return jnp.where(mask, jnp.exp(jnp.where(mask, diff, 0.0)), 0.0)

def ssd_mixer(z, xBC, dt_raw, conv_w, conv_b, dt_bias, A_log, D_skip, norm_g):
    Bsz, S, _ = z.shape
    nc = S // CHUNK
    G, R, P, N = SSD_GROUPS, SSD_HEADS // SSD_GROUPS, SSD_HEAD_DIM, SSD_STATE
    xBC = jax.nn.silu(causal_dwconv(xBC, conv_w, conv_b)).astype(jnp.float32)
    xs, Bm, Cm = jnp.split(xBC, [SSD_D_INNER, SSD_D_INNER + G * N], axis=-1)
    dt = jax.nn.softplus(dt_raw.astype(jnp.float32) + dt_bias.astype(jnp.float32))
    A = -jnp.exp(A_log.astype(jnp.float32))
    x_heads = xs.reshape(Bsz, S, SSD_HEADS, P)
    X = (x_heads * dt[..., None]).reshape(Bsz, nc, CHUNK, G, R, P)
    a = (dt * A).reshape(Bsz, nc, CHUNK, G, R).transpose(0, 3, 4, 1, 2)
    Bc = Bm.reshape(Bsz, nc, CHUNK, G, N)
    Cc = Cm.reshape(Bsz, nc, CHUNK, G, N)
    a_cs = jnp.cumsum(a, axis=-1)
    Lmat = segsum_exp(a)
    CB = jnp.einsum('bclgn,bcsgn->bcgls', Cc, Bc)
    y_diag = jnp.einsum('bcgls,bgrcls,bcsgrp->bclgrp', CB, Lmat, X)
    decay_states = jnp.exp(a_cs[..., -1:] - a_cs)
    states = jnp.einsum('bclgn,bgrcl,bclgrp->bcgrpn', Bc, decay_states, X)
    chunk_decay = jnp.exp(a_cs[..., -1])

    def chunk_step(state, inp):
        st_c, dec_c = inp
        return state * dec_c[..., None, None] + st_c, state

    init = jnp.zeros((Bsz, G, R, P, N), jnp.float32)
    _, prev = lax.scan(chunk_step, init, (jnp.moveaxis(states, 1, 0), jnp.moveaxis(chunk_decay, 3, 0)))
    prev = jnp.moveaxis(prev, 0, 1)
    y_off = jnp.einsum('bclgn,bcgrpn,bgrcl->bclgrp', Cc, prev, jnp.exp(a_cs))
    y = (y_diag + y_off).reshape(Bsz, S, SSD_HEADS, P) + D_skip.astype(jnp.float32)[:, None] * x_heads
    y = y.reshape(Bsz, S, SSD_D_INNER) * jax.nn.silu(z.astype(jnp.float32))
    y = rmsnorm(y.reshape(Bsz, S, G, SSD_D_INNER // G), norm_g.reshape(G, SSD_D_INNER // G))
    return y.reshape(Bsz, S, SSD_D_INNER).astype(z.dtype)

def gla_mixer(q, k, v, r, a1, w_a2, b_a, norm_g):
    Bsz, S, _ = q.shape
    nc = S // CHUNK
    H, dk, dv = GLA_HEADS, GLA_HEAD_K, GLA_HEAD_V
    log_alpha = jax.nn.log_sigmoid((a1 @ w_a2 + b_a).astype(jnp.float32)) / GLA_TAU
    qc = q.astype(jnp.float32).reshape(Bsz, nc, CHUNK, H, dk) * (dk ** -0.5)
    kc = k.astype(jnp.float32).reshape(Bsz, nc, CHUNK, H, dk)
    vc = v.astype(jnp.float32).reshape(Bsz, nc, CHUNK, H, dv)
    bcum = jnp.cumsum(log_alpha.reshape(Bsz, nc, CHUNK, H, dk), axis=2)
    b_last = bcum[:, :, -1:]
    q_t = qc * jnp.exp(bcum)
    k_t = kc * jnp.exp(-bcum)
    k_h = kc * jnp.exp(b_last - bcum)
    mask = jnp.tril(jnp.ones((CHUNK, CHUNK), dtype=bool))
    att = jnp.where(mask, jnp.einsum('bclhd,bcshd->bchls', q_t, k_t), 0.0)
    o_intra = jnp.einsum('bchls,bcshv->bclhv', att, vc)
    U = jnp.einsum('bclhd,bclhv->bchdv', k_h, vc)
    dec = jnp.exp(b_last[:, :, 0])

    def chunk_step(state, inp):
        u_c, d_c = inp
        return state * d_c[..., None] + u_c, state

    init = jnp.zeros((Bsz, H, dk, dv), jnp.float32)
    _, prev = lax.scan(chunk_step, init, (jnp.moveaxis(U, 1, 0), jnp.moveaxis(dec, 1, 0)))
    prev = jnp.moveaxis(prev, 0, 1)
    o_inter = jnp.einsum('bclhd,bchdv->bclhv', q_t, prev)
    o = (o_intra + o_inter).reshape(Bsz, S, H, dv)
    o = rmsnorm(o, norm_g).reshape(Bsz, S, GLA_DV)
    return (o * jax.nn.silu(r.astype(jnp.float32))).astype(q.dtype)

def hybrid_mixer(n, w_in, conv_w, conv_b, dt_bias, A_log, D_skip, ssd_norm,
                 gla_w_a2, gla_b_a, gla_norm, w_up_ssd, w_up_gla, w_o):
    proj = n @ w_in
    idx = np.cumsum(IN_SIZES)[:-1].tolist()
    z, xBC, dt_raw, q, k, v, r, a1, g_ssd, g_gla = jnp.split(proj, idx, axis=-1)
    y_ssd = ssd_mixer(z, xBC, dt_raw, conv_w, conv_b, dt_bias, A_log, D_skip, ssd_norm)
    y_gla = gla_mixer(q, k, v, r, a1, gla_w_a2, gla_b_a, gla_norm)
    merged = jax.nn.sigmoid(g_ssd) * (y_ssd @ w_up_ssd) + jax.nn.sigmoid(g_gla) * (y_gla @ w_up_gla)
    return merged @ w_o

def mem_cross_attention(n, m, w_xq, w_xkv, w_xo):
    Bsz, S, _ = n.shape
    q = (n @ w_xq).reshape(Bsz, S, XATTN_HEADS, XATTN_HEAD_DIM)
    k, v = jnp.split(m @ w_xkv, 2, axis=-1)
    k = k.reshape(Bsz, -1, XATTN_HEADS, XATTN_HEAD_DIM)
    v = v.reshape(Bsz, -1, XATTN_HEADS, XATTN_HEAD_DIM)
    s = jnp.einsum('bshd,bmhd->bhsm', q, k).astype(jnp.float32) * (XATTN_HEAD_DIM ** -0.5)
    p = jax.nn.softmax(s, axis=-1).astype(v.dtype)
    o = jnp.einsum('bhsm,bmhd->bshd', p, v).reshape(Bsz, S, D_MODEL)
    return o @ w_xo

def swiglu(n, w_ffn_in, w_ffn_out):
    g, u = jnp.split(n @ w_ffn_in, 2, axis=-1)
    return (jax.nn.silu(g) * u) @ w_ffn_out

def first_inputs(seed: int = 0) -> dict:
    key = jax.random.key(seed)
    ks = jax.random.split(key, 26)
    f32 = jnp.float32
    L = DEPTH

    def nrm(k, shape, scale):
        return jax.random.normal(k, shape, f32) * scale

    def gain(k, shape):
        return 1.0 + 0.02 * jax.random.normal(k, shape, f32)

    dt = jnp.exp(jax.random.uniform(ks[6], (L, SSD_HEADS), f32, math.log(DT_MIN), math.log(DT_MAX)))
    dt_bias = dt + jnp.log(-jnp.expm1(-dt))
    A_log = jnp.log(jax.random.uniform(ks[7], (L, SSD_HEADS), f32, 1.0, 16.0))
    return {
        "x": jax.random.normal(ks[0], (BATCH, SEQ, D_MODEL), f32),
        "mem": jax.random.normal(ks[1], (BATCH, MEM_LEN, D_MODEL), f32),
        "norm_mix": gain(ks[2], (L, D_MODEL)),
        "w_in": nrm(ks[3], (L, D_MODEL, IN_WIDTH), D_MODEL ** -0.5),
        "ssd_conv_w": nrm(ks[4], (L, SSD_CONV, 1, SSD_CONV_CH), SSD_CONV ** -0.5),
        "ssd_conv_b": nrm(ks[5], (L, SSD_CONV_CH), 0.02),
        "ssd_dt_bias": dt_bias,
        "ssd_A_log": A_log,
        "ssd_D": 1.0 + 0.1 * jax.random.normal(ks[8], (L, SSD_HEADS), f32),
        "ssd_norm": gain(ks[9], (L, SSD_D_INNER)),
        "gla_w_a2": nrm(ks[10], (L, GLA_GATE_RANK, GLA_DK), GLA_GATE_RANK ** -0.5),
        "gla_b_a": nrm(ks[11], (L, GLA_DK), 0.02),
        "gla_norm": gain(ks[12], (L, GLA_HEAD_V)),
        "w_up_ssd": nrm(ks[13], (L, SSD_D_INNER, D_MODEL), SSD_D_INNER ** -0.5),
        "w_up_gla": nrm(ks[14], (L, GLA_DV, D_MODEL), GLA_DV ** -0.5),
        "w_o": nrm(ks[15], (L, D_MODEL, D_MODEL), D_MODEL ** -0.5),
        "norm_xattn": gain(ks[16], (L, D_MODEL)),
        "norm_mem": gain(ks[17], (L, D_MODEL)),
        "w_xq": nrm(ks[18], (L, D_MODEL, D_MODEL), D_MODEL ** -0.5),
        "w_xkv": nrm(ks[19], (L, D_MODEL, 2 * D_MODEL), D_MODEL ** -0.5),
        "w_xo": nrm(ks[20], (L, D_MODEL, D_MODEL), D_MODEL ** -0.5),
        "norm_ffn": gain(ks[21], (L, D_MODEL)),
        "w_ffn_in": nrm(ks[22], (L, D_MODEL, 2 * D_FF), D_MODEL ** -0.5),
        "w_ffn_out": nrm(ks[23], (L, D_FF, D_MODEL), D_FF ** -0.5),
        "norm_final": gain(ks[24], (D_MODEL,)),
    }

def first_block(x, mem, norm_mix, w_in, ssd_conv_w, ssd_conv_b, ssd_dt_bias, ssd_A_log, ssd_D, ssd_norm,
              gla_w_a2, gla_b_a, gla_norm, w_up_ssd, w_up_gla, w_o, norm_xattn, norm_mem, w_xq, w_xkv,
              w_xo, norm_ffn, w_ffn_in, w_ffn_out, norm_final):
    h = x
    for i in range(DEPTH):
        h = h + hybrid_mixer(rmsnorm(h, norm_mix[i]), w_in[i], ssd_conv_w[i], ssd_conv_b[i], ssd_dt_bias[i],
                             ssd_A_log[i], ssd_D[i], ssd_norm[i], gla_w_a2[i], gla_b_a[i], gla_norm[i],
                             w_up_ssd[i], w_up_gla[i], w_o[i])
        h = h + mem_cross_attention(rmsnorm(h, norm_xattn[i]), rmsnorm(mem, norm_mem[i]),
                                    w_xq[i], w_xkv[i], w_xo[i])
        h = h + swiglu(rmsnorm(h, norm_ffn[i]), w_ffn_in[i], w_ffn_out[i])
    return rmsnorm(h, norm_final)


DEPTH_2 = 2

N_META = 16
N_MIXERS = 2
SB_HEADS = 16
SB_HEAD_DIM = D_MODEL // SB_HEADS
Q_BLOCK = 128
LRU_WIDTH = D_MODEL
LRU_BLOCKS = 8
LRU_BLOCK_DIM = LRU_WIDTH // LRU_BLOCKS
CONV_WIDTH = 4
LRU_C = 8.0
D_FF_2 = 4 * D_MODEL
N_SB_LAYERS = (DEPTH_2 + 1) // 2
N_LRU_LAYERS = DEPTH_2 // 2


def rms_norm(x, g):
    xf = x.astype(jnp.float32)
    y = xf * lax.rsqrt(jnp.mean(xf * xf, axis=-1, keepdims=True) + EPS)
    return (y * g.astype(jnp.float32)).astype(x.dtype)

def _sb_block(q_blk, k, v, q_pos):
    t_len = k.shape[2]
    k_pos = jnp.arange(t_len)
    z = jnp.einsum('bhqd,bhkd->bhqk', q_blk, k).astype(jnp.float32) * (SB_HEAD_DIM ** -0.5)
    causal = k_pos[None, :] < q_pos[:, None]
    log_keep = jnp.where(causal, -jax.nn.softplus(z), 0.0)
    after = lax.cumsum(log_keep, axis=3, reverse=True) - log_keep
    w = jnp.where(causal, jnp.exp(jax.nn.log_sigmoid(z) + after), 0.0)
    return jnp.einsum('bhqk,bhkd->bhqd', w.astype(v.dtype), v)

def stick_breaking_mixer(x, w_qkv, w_o):
    b, t_len, _ = x.shape
    qkv = (x @ w_qkv).reshape(b, t_len, 3, SB_HEADS, SB_HEAD_DIM).transpose(2, 0, 3, 1, 4)
    q, k, v = qkv[0], qkv[1], qkv[2]
    meta_out = _sb_block(q[:, :, :N_META], k, v, jnp.arange(N_META))
    n_blk = (t_len - N_META) // Q_BLOCK
    q_real = q[:, :, N_META:].reshape(b, SB_HEADS, n_blk, Q_BLOCK, SB_HEAD_DIM).transpose(2, 0, 1, 3, 4)
    pos = N_META + jnp.arange(n_blk * Q_BLOCK).reshape(n_blk, Q_BLOCK)
    real_out = lax.map(lambda a: _sb_block(a[0], k, v, a[1]), (q_real, pos))
    real_out = real_out.transpose(1, 2, 0, 3, 4).reshape(b, SB_HEADS, n_blk * Q_BLOCK, SB_HEAD_DIM)
    o = jnp.concatenate([meta_out, real_out], axis=2)
    o = o.transpose(0, 2, 1, 3).reshape(b, t_len, D_MODEL)
    return o @ w_o

def _lru_combine(left, right):
    a1, b1 = left
    a2, b2 = right
    return a1 * a2, a2 * b1 + b2

def rglru_mixer(x, w_in, conv_w, conv_b, w_rg, b_rg, w_ig, b_ig, lam, w_out):
    b, t_len, _ = x.shape
    gate_in, rec_in = jnp.split(x @ w_in, 2, axis=-1)
    gate = jax.nn.gelu(gate_in)
    xp = jnp.pad(rec_in, ((0, 0), (CONV_WIDTH - 1, 0), (0, 0)))
    u = conv_b + sum(xp[:, j:j + t_len] * conv_w[j] for j in range(CONV_WIDTH))
    ub = u.reshape(b, t_len, LRU_BLOCKS, LRU_BLOCK_DIM)
    r = jax.nn.sigmoid(jnp.einsum('btni,nij->btnj', ub, w_rg).reshape(b, t_len, LRU_WIDTH) + b_rg)
    i = jax.nn.sigmoid(jnp.einsum('btni,nij->btnj', ub, w_ig).reshape(b, t_len, LRU_WIDTH) + b_ig)
    log_a = (-LRU_C * jax.nn.softplus(-lam.astype(jnp.float32))) * r.astype(jnp.float32)
    a = jnp.exp(log_a)
    mult = jnp.sqrt(-jnp.expm1(2.0 * log_a))
    bt = mult * (i * u).astype(jnp.float32)
    _, h = lax.associative_scan(_lru_combine, (a, bt), axis=1)
    y = h.astype(x.dtype) * gate
    return y @ w_out

def sq_relu_mlp(x, w_up, w_down):
    hdn = jax.nn.relu(x @ w_up)
    return (hdn * hdn) @ w_down

def second_inputs(seed: int = 0) -> dict:
    key = jax.random.key(seed)
    ks = jax.random.split(key, 20)
    f32 = jnp.float32
    D = D_MODEL

    def nrm(k, shape, scale):
        return jax.random.normal(k, shape, f32) * scale

    a0 = jax.random.uniform(ks[11], (N_LRU_LAYERS, LRU_WIDTH), f32, 0.9, 0.999)
    return {
        "x": nrm(ks[0], (BATCH, SEQ, D), 1.0),
        "meta_tokens": nrm(ks[1], (N_META, D), 1.0),
        "norm_mix": 1.0 + nrm(ks[2], (DEPTH_2, D), 0.02),
        "norm_mlp": 1.0 + nrm(ks[3], (DEPTH_2, D), 0.02),
        "sb_w_qkv": nrm(ks[4], (N_SB_LAYERS, D, 3 * D), D ** -0.5),
        "sb_w_o": nrm(ks[5], (N_SB_LAYERS, D, D), D ** -0.5),
        "lru_w_in": nrm(ks[6], (N_LRU_LAYERS, D, 2 * LRU_WIDTH), D ** -0.5),
        "lru_conv_w": nrm(ks[7], (N_LRU_LAYERS, CONV_WIDTH, LRU_WIDTH), CONV_WIDTH ** -0.5),
        "lru_conv_b": nrm(ks[8], (N_LRU_LAYERS, LRU_WIDTH), 0.01),
        "lru_w_rg": nrm(ks[9], (N_LRU_LAYERS, LRU_BLOCKS, LRU_BLOCK_DIM, LRU_BLOCK_DIM), LRU_BLOCK_DIM ** -0.5),
        "lru_b_rg": nrm(ks[10], (N_LRU_LAYERS, LRU_WIDTH), 0.01),
        "lru_w_ig": nrm(ks[12], (N_LRU_LAYERS, LRU_BLOCKS, LRU_BLOCK_DIM, LRU_BLOCK_DIM), LRU_BLOCK_DIM ** -0.5),
        "lru_b_ig": nrm(ks[13], (N_LRU_LAYERS, LRU_WIDTH), 0.01),
        "lru_lambda": jnp.log(a0) - jnp.log1p(-a0),
        "lru_w_out": nrm(ks[14], (N_LRU_LAYERS, LRU_WIDTH, D), LRU_WIDTH ** -0.5),
        "mlp_w_up": nrm(ks[15], (DEPTH_2, D, D_FF_2), D ** -0.5),
        "mlp_w_down": nrm(ks[16], (DEPTH_2, D_FF_2, D), D_FF_2 ** -0.5),
        "norm_final": 1.0 + nrm(ks[17], (D,), 0.02),
    }

def second_block(x, meta_tokens, norm_mix, norm_mlp, sb_w_qkv, sb_w_o, lru_w_in, lru_conv_w,
              lru_conv_b, lru_w_rg, lru_b_rg, lru_w_ig, lru_b_ig, lru_lambda, lru_w_out,
              mlp_w_up, mlp_w_down, norm_final):
    b = x.shape[0]
    meta = jnp.broadcast_to(meta_tokens[None].astype(x.dtype), (b, N_META, D_MODEL))
    h = jnp.concatenate([meta, x], axis=1)
    for i in range(DEPTH_2):
        hn = rms_norm(h, norm_mix[i])
        j = i // N_MIXERS
        if i % N_MIXERS == 0:
            h = h + stick_breaking_mixer(hn, sb_w_qkv[j], sb_w_o[j])
        else:
            h = h + rglru_mixer(hn, lru_w_in[j], lru_conv_w[j], lru_conv_b[j], lru_w_rg[j],
                                lru_b_rg[j], lru_w_ig[j], lru_b_ig[j], lru_lambda[j], lru_w_out[j])
        hn = rms_norm(h, norm_mlp[i])
        h = h + sq_relu_mlp(hn, mlp_w_up[i], mlp_w_down[i])
    h = rms_norm(h, norm_final)
    return h[:, N_META:]


def setup_inputs(seed=0):
    out = dict(first_inputs(seed))
    for name, value in second_inputs(seed + 1).items():
        if name != "x":
            out[name + "_2"] = value
    return out


def reference(
    x, mem, norm_mix, w_in, ssd_conv_w, ssd_conv_b, ssd_dt_bias, ssd_A_log, ssd_D, ssd_norm,
    gla_w_a2, gla_b_a, gla_norm, w_up_ssd, w_up_gla, w_o, norm_xattn, norm_mem, w_xq, w_xkv,
    w_xo, norm_ffn, w_ffn_in, w_ffn_out, norm_final, meta_tokens_2, norm_mix_2, norm_mlp_2,
    sb_w_qkv_2, sb_w_o_2, lru_w_in_2, lru_conv_w_2, lru_conv_b_2, lru_w_rg_2, lru_b_rg_2,
    lru_w_ig_2, lru_b_ig_2, lru_lambda_2, lru_w_out_2, mlp_w_up_2, mlp_w_down_2, norm_final_2,
):
    x = first_block(
        x, mem, norm_mix, w_in, ssd_conv_w, ssd_conv_b, ssd_dt_bias, ssd_A_log, ssd_D, ssd_norm,
        gla_w_a2, gla_b_a, gla_norm, w_up_ssd, w_up_gla, w_o, norm_xattn, norm_mem, w_xq, w_xkv,
        w_xo, norm_ffn, w_ffn_in, w_ffn_out, norm_final,
    )
    return second_block(
        x, meta_tokens_2, norm_mix_2, norm_mlp_2, sb_w_qkv_2, sb_w_o_2, lru_w_in_2,
        lru_conv_w_2, lru_conv_b_2, lru_w_rg_2, lru_b_rg_2, lru_w_ig_2, lru_b_ig_2,
        lru_lambda_2, lru_w_out_2, mlp_w_up_2, mlp_w_down_2, norm_final_2,
    )


_drawn_inputs = setup_inputs


def setup_inputs(seed=0):
    import zlib

    import numpy as np

    out = dict(_drawn_inputs(seed))
    spreads = {}
    factors = {'ssd_conv_b': 3.063,
     'ssd_norm': 4.524,
     'gla_b_a': 8.0,
     'gla_norm': 7.939,
     'norm_xattn': 8.0,
     'norm_mem': 8.0,
     'norm_ffn': 3.404,
     'norm_mix_2': 3.08,
     'lru_conv_b_2': 23.107,
     'lru_b_rg_2': 114.941,
     'lru_b_ig_2': 29.187,
     'norm_final_2': 23.511,
     'norm_mlp_2': 4.298}
    for name, (base, spread) in spreads.items():
        noise = np.random.default_rng([zlib.crc32(name.encode()), seed]).standard_normal(out[name].shape)
        drawn = base * np.exp(spread * noise) if base else spread * noise
        out[name] = __import__('jax').numpy.asarray(drawn.astype(out[name].dtype))
    for name, factor in factors.items():
        out[name] = (out[name] * factor).astype(out[name].dtype)
    return out
```

```python
from contextlib import ExitStack

import concourse.bass as bass
from concourse import mybir

P = 128
F32 = mybir.dt.float32
F32R = mybir.dt.float32r
BF16 = mybir.dt.bfloat16
ALU = mybir.AluOpType
ACT = mybir.ActivationFunctionType
AX = mybir.AxisListType.X

D = 1024
KB = D // P
T1 = 256
META = 16
T2 = T1 + META
EPS = 1e-6
CHUNK = 64
NCH = T1 // CHUNK
SSD_HEADS = 16
GLA_HEADS = 4
XH = 4
SBH = 16
FFN_KB = 22
MLP_KB = 32
RING = 4
BIG = 1e30
KPAD = 3 * P
ZC = T2 + (T2 - P) + META

PHASES = [
    ("xbc", 12, 12), ("q", 4, 4), ("k", 4, 4), ("v", 8, 8), ("z", 8, 8), ("r", 8, 8), ("gs", 8, 8),
    ("gg", 8, 8), ("ups", 8, 8), ("upg", 8, 8), ("wo", 8, 8), ("xk", 8, 8), ("xq", 8, 8), ("xv", 8, 8),
    ("xo", 8, 8), ("ffi", 44, 44), ("ffo", 22, 8), ("sq", 8, 8), ("sk", 8, 8), ("sv", 8, 8),
    ("so", 8, 8), ("up0", 32, 32), ("dn0", 32, 8), ("rec", 8, 8), ("rgig", 2, 16), ("gate", 8, 8),
    ("lo", 8, 8), ("up1", 32, 32), ("dn1", 32, 8),
]
UNITS = {}
OUTS = {}
_u = _e = 0
for _name, _n, _o in PHASES:
    UNITS[_name], OUTS[_name] = (_u, _n), _e
    _u += _n
    _e += _o
NU = _u

MISC = ["st_mix", "small", "gate0", "gate1", "ctok", "cb0", "cb1", "xt0", "xt1", "xt2", "xt3",
        "kht0", "kht1", "att0", "att1", "u0", "u1", "u2", "u3", "u4", "u5", "o0", "o1", "st_ssd", "o2", "o3",
        "st_gla0", "st_gla1", "st_mem", "st_xattn", "pt0", "pt1", "pt2", "pt3",
        "st_ffn", "st_fin1", "st_sb", "st_mlp0", "st_lru", "st_mlp1", "st_fin2"]
R = {name: n for n, name in enumerate(MISC)}
GROUPS = [(("gate0", "gate1"), (3, 0)),
          (("cb0", "cb1", "xt0", "xt1", "xt2", "xt3"), (3, 0, 1, 2, 3, 2))]
BANK = {name: 3 for name in MISC}
FREE = dict(R)
for _names, _banks in GROUPS:
    for _i, _name in enumerate(_names):
        BANK[_name] = _banks[_i]
        FREE[_name] = max([R[_names[0]]] + [R[_names[_j]] + 1 for _j in range(_i) if _banks[_j] == _banks[_i]])

OPER = {name: n for n, name in enumerate(["mix", "xattn", "ffn", "sb", "mlp0", "lru", "mlp1"])}
STAT = {name: n for n, name in enumerate(["mix", "xattn", "ffn", "fin1", "sb", "mlp0", "lru", "mlp1", "fin2"])}

PARAMS = [("mix", 8), ("mem", 8), ("xattn", 8), ("ffn", 8), ("fin1", 8), ("sb", 8), ("mlp0", 8),
          ("lru", 8), ("mlp1", 8), ("fin2", 8), ("convw", 48), ("convb", 12), ("dskip", 8),
          ("ssdn", 8), ("glan", 2), ("glab", 4), ("dtb", 1), ("alog", 1), ("lconvw", 32),
          ("lconvb", 8), ("brg", 8), ("big", 8), ("lam", 8)]
PC = {}
_c = 0
for _name, _n in PARAMS:
    PC[_name] = _c
    _c += _n
NPAR = _c
CONV_AT = [c + c // 2 + 1 for c in range(12)]
SILU_AT = [11 + 2 * c // 3 for c in range(12)]


def blk(t, b, lo, hi):
    if isinstance(b, int):
        return t[:, b, lo:hi]
    return t[:, bass.ds(b, 1), lo:hi].rearrange("p o n -> p (o n)")


def col(t, c):
    if isinstance(c, int):
        return t[:, c:c + 1]
    return t[:, bass.ds(c, 1)]


def blocks_kernel(nc, w, wsmall, wa2, par, xT, memT, metaT, out):
    with ExitStack() as ctx:
        def sb(name, shape, dt=F32, stack=ctx):
            return stack.enter_context(nc.sbuf_tensor(name, shape, dt))

        def sem(name):
            return ctx.enter_context(nc.semaphore(name))

        raw = sb("raw", [P, RING, 1024])
        whi = sb("whi", [P, RING, KB, P], F32R)
        wlo = sb("wlo", [P, RING, KB, P], F32R)
        hT = sb("hT", [P, KB, T2])
        xh = sb("xh", [P, KB, T2], F32R)
        xl = sb("xl", [P, KB, T2], F32R)
        yh = sb("yh", [P, KB, T2], F32R)
        yl = sb("yl", [P, KB, T2], F32R)
        sq = sb("sq", [P, KB, T2])
        pr = sb("pr", [P, NPAR])
        ident = sb("ident", [P, P])
        mean1024 = sb("mean1024", [P, P])
        mean512 = sb("mean512", [P, P])
        mean256 = sb("mean256", [P, P])
        ones = sb("ones", [P, P])
        tri = sb("tri", [P, P])
        identb = sb("identb", [P, P], BF16)
        bigm = sb("bigm", [P, P], BF16)
        rt = sb("rt", [P, T2])
        rstd = sb("rstd", [P, T2])
        rstdh = sb("rstdh", [P, T2])
        rtt = sb("rtt", [P, 3])
        rtok = sb("rtok", [P, 3])
        t4 = sb("t4", [P, 4, T2])

        small = sb("small", [P, 96])
        halfc = small[:, 0:60]
        expa = small[0:16, 60:61]
        dec = small[:, 64:80].rearrange("p (h c) -> p h c", h=4)


        s1 = ExitStack()
        convin = sb("convin", [P, 12, 3 + T1], stack=s1)
        xc = sb("xc", [P, 12, T1], stack=s1)
        qf = sb("qf", [P, 4, T1], stack=s1)
        kf = sb("kf", [P, 4, T1], stack=s1)
        kt = sb("kt", [P, 4, T1], stack=s1)
        bcn = sb("bcn", [P, 4, T1], stack=s1)
        etmp = sb("etmp", [P, 4, T1], stack=s1)
        khk = sb("khk", [P, 2, 512], stack=s1)
        vt = sb("vt", [P, 2, D], stack=s1)
        sz = sb("sz", [P, KB, T1], stack=s1)
        sr = sb("sr", [P, KB, T1], stack=s1)
        sg1 = sb("sg1", [P, KB, T1], stack=s1)
        sg2 = sz
        xk_ = sb("xdt", [P, 2, D], stack=s1)
        csn = sb("csn", [16, 384], stack=s1)
        ctok = sb("ctok", [P, 4, 16], stack=s1)
        wsh = sb("wsh", [P, KB, 48], F32R, stack=s1)
        wsl = sb("wsl", [P, KB, 48], F32R, stack=s1)
        flat = xk_[:, :, :].rearrange("p a b -> p (a b)")
        smt, xdt, adt, one16, lnb = [flat[:, 256 * n:256 * n + 256] for n in range(5)]
        wsr = flat[:, 1280:1664]
        dtT = flat[:, 1664:1920]
        wa = bcn[:, :, :].rearrange("p a b -> p (a b)")[:, 0:512]
        cflat = convin[:, :, :].rearrange("p a b -> p (a b)")
        y = cflat[:, 0:2048].rearrange("p (b t) -> p b t", b=KB)
        att = cflat[:, 2048:3072].rearrange("p (t h l) -> p t h l", t=2, h=4)
        state = (kf, bcn, etmp)
        o = flat.rearrange("p (b t) -> p b t", b=KB)
        sflat = sq[:, :, :].rearrange("p a b -> p (a b)")
        CB = sflat[:, 0:768].rearrange("p (g l) -> p g l", g=2)
        L = sflat[:, 768:1920].rearrange("p (n l) -> p n l", n=3)
        ry = kt[:, 0:2, :]
        ro = khk[:, :, :].rearrange("p a b -> p (a b)").rearrange("p (h t) -> p h t", h=4)
        s1.close()

        s2 = ExitStack()
        mem = sb("mem", [P, KB, T1], stack=s2)
        memsq = sb("memsq", [P, KB, T1], stack=s2)
        memh = sb("memh", [P, KB, T1], F32R, stack=s2)
        meml = sb("meml", [P, KB, T1], F32R, stack=s2)
        xkT = sb("xkT", [P, KB, T1], stack=s2)
        xqT = sb("xqT", [P, KB, T1], stack=s2)
        xv = sb("xv", [P, 2, D], stack=s2)
        prob = sb("prob", [P, 2, 2, T1], stack=s2)
        probT = sb("probT", [P, XH, 2, T1], stack=s2)
        mx = sb("mx", [P, XH, 2], stack=s2)
        sums = sb("sums", [P, XH, 2], stack=s2)
        rsum = sb("rsum", [P, XH, 2], stack=s2)
        rstdm = sb("rstdm", [P, T1], stack=s2)
        s2.close()

        s3 = ExitStack()
        hh = sb("hh", [P, MLP_KB, T2], F32R, stack=s3)
        hl = sb("hl", [P, MLP_KB, T2], F32R, stack=s3)
        s3.close()

        s4 = ExitStack()
        sqT = sb("sqT", [P, KB, T2], stack=s4)
        skT = sb("skT", [P, KB, KPAD], stack=s4)
        sv = sb("sv", [P, 3, D], stack=s4)
        sp = sb("sp", [P, 4, ZC], stack=s4)
        lk = sb("lk", [P, 2, ZC], stack=s4)
        wT = sb("wT", [P, 2, ZC], stack=s4)
        nmask = sb("nmask", [P, ZC], stack=s4)
        bmask = sb("bmask", [P, ZC], stack=s4)
        s4.close()

        s5 = ExitStack()
        recin = sb("recin", [P, KB, 3 + T2], stack=s5)
        uu = sb("uu", [P, KB, T2], stack=s5)
        uh = sb("uh", [P, KB, T2], F32R, stack=s5)
        ul = sb("ul", [P, KB, T2], F32R, stack=s5)
        thr = sb("thr", [P, KB, T2], stack=s5)
        thi = sb("thi", [P, KB, T2], stack=s5)
        aa = sb("aa", [P, KB, T2], stack=s5)
        gg = sb("gg", [P, KB, T2], stack=s5)
        half = sb("half", [P, 32], stack=s5)
        s5.close()
        acc = ctx.enter_context(nc.psum_tensor("acc", [P, 4, 512], F32))
        mix = ctx.enter_context(nc.psum_tensor("mix", [P, 4, 512], F32))
        zbank = [mix[:, 0, :], mix[:, 1, :], mix[:, 3, :], acc[:, 0, :]]
        obank = [mix[:, 2, :], acc[:, 1, :]]
        MISCB = 3

        landed = [sem(f"landed{j}") for j in range(RING)]
        hi_ready, lo_ready, unit_done = sem("hi_ready"), sem("lo_ready"), sem("unit_done")
        evacuated = [sem(f"evacuated{j}") for j in range(4)]
        misc_ready, misc_free = sem("misc_ready"), sem("misc_free")
        head_ready, head_free = sem("head_ready"), sem("head_free")
        y_ready, y_free = sem("y_ready"), sem("y_free")
        consts = sem("consts")
        par_in, x_in, meta_in, ws_in, wa_in, mem_in = [sem(n) for n in
            ("par_in", "x_in", "meta_in", "ws_in", "wa_in", "mem_in")]
        xh_ready, xl_ready, sq_ready = sem("xh_ready"), sem("xl_ready"), sem("sq_ready")
        rstd_ready, rstdh_ready = sem("rstd_ready"), sem("rstdh_ready")
        ws_ready, wsl_ready = sem("ws_ready"), sem("wsl_ready")
        th_ready, silu_done = sem("th_ready"), sem("silu_done")
        conv_step, conv_th, conv_out = sem("conv_step"), sem("conv_th"), sem("conv_out")
        dt_step, dt_act = sem("dt_step"), sem("dt_act")
        gla_step, gla_act = sem("gla_step"), sem("gla_act")
        M_ready, att_sel = sem("M_ready"), sem("att_sel")
        n_sq, n_r, n_y, o_step = sem("n_sq"), sem("n_r"), sem("n_y"), sem("o_step")
        yh_ready, yl_ready, merged = sem("yh_ready"), sem("yl_ready"), sem("merged")
        memh_ready, meml_ready, memsq_ready = sem("memh_ready"), sem("meml_ready"), sem("memsq_ready")
        sm_step, pv_done = sem("sm_step"), sem("pv_done")
        hid_ready, hh_ready, hl_ready = sem("hid_ready"), sem("hh_ready"), sem("hl_ready")
        sbmask, sb_act, lk_step, tri_ready, wT_ready = [sem(n) for n in
            ("sbmask", "sb_act", "lk_step", "tri_ready", "wT_ready")]
        fin_step, out_done = sem("fin_step"), sem("out_done")
        lru_step, lru_act, lru_done, uh_ready, ul_ready, lru_zero, lam_step = [sem(n) for n in
            ("lru_step", "lru_act", "lru_done", "uh_ready", "ul_ready", "lru_zero", "lam_step")]

        def g(name, b=0):
            return col(pr, PC[name] + b)

        block = ctx.enter_context(nc.Block())

        @block.sync
        def _(sp_):
            for j in range(RING):
                sp_.dma_start(raw[:, j, :], w[j, :, :]).then_inc(landed[j], 16)
            with sp_.Fori(1, NU // RING) as i:
                for j in range(RING):
                    sp_.wait_ge(lo_ready, 4 * i + (j - 3))
                    sp_.dma_start(raw[:, j, :], w[bass.ds(4 * i + j, 1), :, :].rearrange("o p n -> (o p) n"))\
                       .then_inc(landed[j], 16)
            for b in range(KB):
                sp_.wait_ge(fin_step, KB + b + 1)
                sp_.dma_start(out[:, b, :], hT[:, b, META:T2]).then_inc(out_done, 16)
            sp_.wait_ge(out_done, 16 * KB)

        @block.gpsimd
        def _(pool):
            for tile, value in ((ident, 0.0), (mean1024, 1.0 / D), (mean512, 1.0 / 512), (mean256, 1.0 / 256),
                                (ones, 1.0), (tri, 1.0), (identb, 0.0), (bigm, 0.0)):
                pool.memset(tile[:, :], value).then_inc(consts, 1)
            pool.memset(convin[:, :, 0:3], 0.0).then_inc(consts, 1)
            pool.memset(kt[:, :, :], 1.0).then_inc(consts, 1)
            pool.memset(one16[0:16, :], 1.0).then_inc(consts, 1)
            pool.wait_ge(consts, 11)
            ktc = kt[:, :, :].rearrange("p a (c s) -> p (a c) s", s=CHUNK)
            pool.memset(ktc[:, :, 0:1], 0.0).then_inc(consts, 1)
            for tile in (ident, identb):
                pool.affine_select(out=tile[:, :], in_=tile[:, :], compare_op=ALU.not_equal, fill=1.0, base=0,
                                   pattern=[[-1, P]], channel_multiplier=1).then_inc(consts, 1)
            pool.affine_select(out=tri[:, :], in_=tri[:, :], compare_op=ALU.is_ge, fill=0.0, base=0,
                               pattern=[[-1, P]], channel_multiplier=1).then_inc(consts, 1)
            pool.affine_select(out=bigm[:, :], in_=bigm[:, :], compare_op=ALU.is_ge, fill=BIG, base=0,
                               pattern=[[1, P]], channel_multiplier=-1).then_inc(consts, 1)
            def masked_decay(h):
                if h == 0:
                    pool.wait_ge(misc_free, R["cb1"] + 1)
                pool.wait_ge(head_free, h + 1)
                pool.tensor_tensor(L[:, h % 3, :], L[:, h % 3, :], CB[:, h // 8, :], ALU.mult).then_inc(M_ready, 1)

            for h in range(10):
                masked_decay(h)
            for t in range(2):
                pool.wait_ge(misc_free, R[f"att{t}"] + 1)
                a = att[:, t, :, :]
                pool.affine_select(out=a, in_=a, compare_op=ALU.is_ge, fill=0.0, base=0,
                                   pattern=[[0, 4], [1, P]], channel_multiplier=-1).then_inc(att_sel, 1)
                pool.wait_ge(att_sel, 2 * t + 1)
                pool.affine_select(out=a[:, :, CHUNK:P], in_=a[:, :, CHUNK:P], compare_op=ALU.is_ge, fill=0.0,
                                   base=-CHUNK, pattern=[[0, 4], [0, CHUNK]], channel_multiplier=1)\
                    .then_inc(att_sel, 1)
                for h in ((10, 11), (12, 13, 14, 15))[t]:
                    masked_decay(h)
            for b in range(KB):
                pool.wait_ge(yh_ready, b + 1)
                pool.tensor_tensor(yl[:, b, 0:T1], y[:, b, :], yh[:, b, 0:T1].bitcast(F32), ALU.subtract)\
                    .then_inc(yl_ready, 1)
            pool.wait_ge(unit_done, UNITS["sq"][0])
            pool.memset(skT[:, :, T2:KPAD], 0.0).then_inc(sbmask, 1)
            pool.memset(nmask[:, :], -1.0).then_inc(sbmask, 1)
            pool.memset(bmask[:, :], 0.0).then_inc(sbmask, 1)
            pool.wait_ge(sbmask, 3)
            for at, n in ((0, T2), (T2, T2 - P), (2 * T2 - P, META)):
                for tile, fill in ((nmask, 0.0), (bmask, -BIG)):
                    pool.affine_select(out=tile[:, at:at + n], in_=tile[:, at:at + n], compare_op=ALU.is_gt,
                                       fill=fill, base=0, pattern=[[1, n]], channel_multiplier=-1)\
                        .then_inc(sbmask, 1)
            pool.wait_ge(unit_done, UNITS["rec"][0])
            pool.memset(recin[:, :, 0:3], 0.0).then_inc(lru_zero, 1)

        @block.tensor
        def _(pe):
            def products(dst, slot, n, rh, rl, first, last):
                nc.tensor.matmul(dst, whi[:, slot, n, :], rh, start=first, stop=False)
                nc.tensor.matmul(dst, whi[:, slot, n, :], rl, start=False, stop=False)
                return nc.tensor.matmul(dst, wlo[:, slot, n, :], rh, start=False, stop=last)

            def unit(phase, m, j, ah, al, T, turn=None, ready=None):
                u0, e0 = UNITS[phase][0], OUTS[phase]
                pe.wait_ge(lo_ready, m + (u0 + 1))
                if turn is None:
                    if (e0 + m) // 4:
                        pe.wait_ge(evacuated[j], (e0 + m) // 4)
                else:
                    pe.wait_ge(evacuated[j], turn + e0 // 4)
                for k in range(KB):
                    if ready is not None:
                        pe.wait_ge(ready[0], ready[1] + k + 1)
                    last = products(acc[:, j, 0:T], (u0 + j) % 4, k, ah[:, k, 0:T], al[:, k, 0:T],
                                    k == 0, k == KB - 1)
                last.then_inc(unit_done, 1)

            def project(phase, ah, al, T, ready=None):
                with pe.Fori(0, UNITS[phase][1] // 4) as i:
                    for j in range(4):
                        unit(phase, 4 * i + j, j, ah, al, T, turn=i, ready=ready if j == 0 else None)

            def token_pair(phase, m, ah, al, tiles):
                u0, e0 = UNITS[phase][0], OUTS[phase]
                pe.wait_ge(lo_ready, u0 + m + 2)
                s = (u0 + m) % 4
                for t, (at, n) in enumerate(tiles):
                    bank = m % 4 + t % 2
                    if t < 2:
                        pe.wait_ge(evacuated[bank], (e0 + m) // 4)
                    dst = acc[0:n, bank, 256 * (t // 2):256 * (t // 2) + 256].rearrange("p (a c) -> p a c", a=2)
                    for k in range(KB):
                        nc.tensor.matmul(dst, ah[:, k, at:at + n], whi[:, s:s + 2, k, :], start=k == 0, stop=False)
                        nc.tensor.matmul(dst, ah[:, k, at:at + n], wlo[:, s:s + 2, k, :], start=False, stop=False)
                        last = nc.tensor.matmul(dst, al[:, k, at:at + n], whi[:, s:s + 2, k, :],
                                                start=False, stop=k == KB - 1)
                last.then_inc(unit_done, 2)

            def misc_bank(name):
                if FREE[name]:
                    pe.wait_ge(misc_free, FREE[name])
                return mix[:, BANK[name], :]

            def mean_squares(name, src, src_ready, base, T, tiles=()):
                dst = misc_bank(name)
                for b in range(KB):
                    pe.wait_ge(src_ready, base + b + 1)
                    last = nc.tensor.matmul(dst[:, 0:T], mean1024[:, :], src[:, b, 0:T], start=b == 0, stop=b == KB - 1)
                for t, (at, n) in enumerate(tiles):
                    for b in range(KB):
                        last = nc.tensor.matmul(dst[0:n, 300 + t:301 + t], src[:, b, at:at + n], mean1024[:, 0:1],
                                                start=b == 0, stop=b == KB - 1)
                last.then_inc(misc_ready, 1)

            def stream_stats(stat, T, tiles=()):
                mean_squares("st_" + stat, sq, sq_ready, KB * STAT[stat], T, tiles)

            def operand(norm):
                return xl_ready, KB * OPER[norm]

            tiles1, tiles2 = [(0, P), (P, P)], [(0, P), (P, P), (2 * P, META)]

            def small_products():
                pe.wait_ge(wsl_ready, 1)
                dst = misc_bank("small")
                for k in range(KB):
                    nc.tensor.matmul(dst[0:48, 0:T1], wsh[:, k, :], xh[:, k, 0:T1], start=k == 0, stop=False)
                    nc.tensor.matmul(dst[0:48, 0:T1], wsh[:, k, :], xl[:, k, 0:T1], start=False, stop=False)
                    last = nc.tensor.matmul(dst[0:48, 0:T1], wsl[:, k, :], xh[:, k, 0:T1], start=False,
                                            stop=k == KB - 1)
                last.then_inc(misc_ready, 1)

            def gla_gates(n):
                dst = misc_bank(f"gate{n}")
                pe.wait_ge(wa_in, 16)
                for i in range(2):
                    f = (2 * n + i) * P
                    last = nc.tensor.matmul(dst[:, 256 * i:256 * i + 256], wa[32:48, f:f + P], smt[32:48, :],
                                            start=True, stop=True)
                last.then_inc(misc_ready, 1)

            def dt_by_token():
                dst = misc_bank("ctok")
                pe.wait_ge(dt_step, 5)
                for n, src in enumerate((csn[:, 0:P], csn[:, P:2 * P], dtT[0:16, 0:P], dtT[0:16, P:2 * P])):
                    last = nc.tensor.transpose(dst[:, 16 * n:16 * n + 16], src, ident[0:16, 0:16])
                last.then_inc(misc_ready, 1)

            def cb(grp):
                dst = misc_bank(f"cb{grp}")
                pe.wait_ge(conv_out, 12)
                nc.tensor.matmul(dst[:, 0:256], xc[:, 8 + grp, 0:P], xc[:, 10 + grp, :], start=True, stop=True)
                nc.tensor.matmul(dst[:, 256:384], xc[:, 8 + grp, P:2 * P], xc[:, 10 + grp, P:2 * P],
                                 start=True, stop=True).then_inc(misc_ready, 1)

            def x_by_token(n):
                t, hf = divmod(n, 2)
                dst = misc_bank(f"xt{n}")
                for i in range(4):
                    last = nc.tensor.transpose(dst[:, P * i:P * i + P], xc[:, 4 * hf + i, P * t:P * t + P], ident[:, :])
                last.then_inc(misc_ready, 1)

            def decay_row(h):
                if h >= 2:
                    pe.wait_ge(head_free, h - 1)
                else:
                    pe.wait_ge(misc_free, R["xt0"] + 1)
                dst = mix[:, h % 2, :]
                sel = ident[0:16, h:h + 1].broadcast_to([16, P])
                nc.tensor.matmul(dst[:, 0:384], sel, csn[:, :], start=True, stop=False)
                nc.tensor.matmul(dst[:, 0:P], identb[:, :], bigm[:, :], start=False, stop=False)
                nc.tensor.matmul(dst[:, 256:384], identb[:, :], bigm[:, :], start=False, stop=True)\
                    .then_inc(head_ready, 1)

            def ssd_out(j):
                if j:
                    pe.wait_ge(y_free, j)
                else:
                    pe.wait_ge(misc_free, R["xt3"] + 1)
                pe.wait_ge(M_ready, 2 * j + 2)
                for h in (2 * j, 2 * j + 1):
                    po, buf = 64 * (h % 2), h % 3
                    nc.tensor.matmul(mix[po:po + 64, 2, 0:256], xk_[:, 0, 64 * h:64 * h + 64], L[:, buf, 0:256],
                                     start=True, stop=False)
                    last = nc.tensor.matmul(mix[po:po + 64, 2, P:256], xk_[:, 1, 64 * h:64 * h + 64],
                                            L[:, buf, 256:384], start=False, stop=True)
                last.then_inc(y_ready, 1)

            def kh_by_token(t):
                dst = misc_bank(f"kht{t}")
                pe.wait_ge(gla_step, 6)
                for h in range(GLA_HEADS):
                    last = nc.tensor.transpose(dst[:, P * h:P * h + P], etmp[:, h, P * t:P * t + P], ident[:, :])
                last.then_inc(misc_ready, 1)

            def gla_scores(t):
                dst = misc_bank(f"att{t}")
                for h in range(GLA_HEADS):
                    last = nc.tensor.matmul(dst[:, P * h:P * h + P], kt[:, h, P * t:P * t + P],
                                            qf[:, h, P * t:P * t + P], start=True, stop=True)
                last.then_inc(misc_ready, 1)

            def chunk_update(n):
                c, hp = divmod(n, 2)
                po = CHUNK * (c % 2)
                dst = misc_bank(f"u{n}")
                for i in range(2):
                    h = 2 * hp + i
                    last = nc.tensor.matmul(dst[:, 256 * i:256 * i + 256], khk[po:po + CHUNK, c // 2, P * h:P * h + P],
                                            vt[po:po + CHUNK, c // 2, 256 * h:256 * h + 256], start=True, stop=True)
                last.then_inc(misc_ready, 1)

            def gla_out(h):
                dst = misc_bank(f"o{h}")
                pe.wait_ge(att_sel, 4)
                for vb in range(2):
                    at = 256 * vb
                    vc = 256 * h + P * vb
                    for t in range(2):
                        nc.tensor.matmul(dst[:, at + P * t:at + P * t + P], vt[:, t, vc:vc + P], att[:, t, h, :],
                                         start=vb == 0 and t == 0, stop=False)
                    for c in range(1, NCH):
                        last = nc.tensor.matmul(dst[:, at + CHUNK * c:at + CHUNK * c + CHUNK],
                                                state[c - 1][:, h, P * vb:P * vb + P],
                                                qf[:, h, CHUNK * c:CHUNK * c + CHUNK],
                                                start=False, stop=vb == 1 and c == NCH - 1)
                last.then_inc(misc_ready, 1)

            unit("xbc", 0, 0, xh, xl, T1, ready=(xl_ready, 0))
            pe.wait_ge(consts, 16)
            stream_stats("mix", T1, tiles1)
            unit("xbc", 1, 1, xh, xl, T1)
            small_products()
            m = 0
            for phase, count in (("xbc", 12), ("q", 4), ("k", 4), ("v", 8), ("z", 8), ("r", 8), ("gs", 8), ("gg", 8)):
                for n in range(count):
                    if phase == "v":
                        if n % 2:
                            token_pair(phase, n - 1, xh, xl, tiles1)
                    elif m > 1:
                        unit(phase, n, n % 4, xh, xl, T1)
                    if m == 3:
                        gla_gates(0)
                        gla_gates(1)
                    if m == 5:
                        dt_by_token()
                    if m == 21:
                        cb(0)
                        cb(1)
                        x_by_token(0)
                        x_by_token(1)
                    if m == 23:
                        x_by_token(2)
                        x_by_token(3)
                    if m >= 27 and m % 2 and m <= 43:
                        j = (m - 27) // 2
                        if j < 8:
                            decay_row(2 * j)
                            decay_row(2 * j + 1)
                        if j:
                            ssd_out(j - 1)
                    if m in (30, 32):
                        kh_by_token((m - 30) // 2)
                    if m in (34, 36):
                        gla_scores((m - 34) // 2)
                    if 38 <= m < 44:
                        chunk_update(m - 38)
                    if m in (44, 45, 48, 49):
                        gla_out((44, 45, 48, 49).index(m))
                    if m == 47:
                        dst = misc_bank("st_ssd")
                        for grp in range(2):
                            for b in range(4):
                                pe.wait_ge(n_sq, 4 * grp + b + 1)
                                last = nc.tensor.matmul(dst[:, 256 * grp:256 * grp + 256], mean512[:, :],
                                                        sq[:, 4 * grp + b, 0:T1], start=b == 0, stop=b == 3)
                        last.then_inc(misc_ready, 1)
                    if m in (52, 54):
                        i = (m - 52) // 2
                        dst = misc_bank(f"st_gla{i}")
                        for hd in range(2):
                            for vb in range(2):
                                b = 4 * i + 2 * hd + vb
                                pe.wait_ge(n_sq, 8 + 2 * i + hd + 1)
                                last = nc.tensor.matmul(dst[:, 256 * hd:256 * hd + 256], mean256[:, :], sq[:, b, 0:T1],
                                                        start=vb == 0, stop=vb == 1)
                        last.then_inc(misc_ready, 1)
                    m += 1

            project("ups", yh, yl, T1, (yl_ready, 0))
            project("upg", xh, xl, T1, (yl_ready, 8))
            project("wo", yh, yl, T1, (yl_ready, 16))

            mean_squares("st_mem", memsq, memsq_ready, 0, T1, tiles1)
            project("xk", memh, meml, T1, (meml_ready, 0))
            stream_stats("xattn", T1)
            project("xq", xh, xl, T1, operand("xattn"))

            def scores(h):
                pe.wait_ge(head_free, SSD_HEADS + h - 1)
                for i in range(2):
                    pe.wait_ge(evacuated[(2 * h + i) % 4], (OUTS["xq"] + 2 * h + i) // 4 + 1)
                for t in range(2):
                    for i in range(2):
                        last = nc.tensor.matmul(mix[:, h % 2, 256 * t:256 * t + 256],
                                                xqT[:, 2 * h + i, P * t:P * t + P], xkT[:, 2 * h + i, :],
                                                start=i == 0, stop=i == 1)
                last.then_inc(head_ready, 1)

            scores(0)
            scores(1)
            for p in range(XH):
                token_pair("xv", 2 * p, memh, meml, tiles1)
                dst = misc_bank(f"pt{p}")
                pe.wait_ge(sm_step, 4 * p + 4)
                for mt in range(2):
                    for t in range(2):
                        last = nc.tensor.transpose(dst[:, 256 * mt + P * t:256 * mt + P * t + P],
                                                   prob[:, p % 2, t, P * mt:P * mt + P], ident[:, :])
                last.then_inc(misc_ready, 1)
                if p < 2:
                    scores(p + 2)
            for h in range(XH):
                if h:
                    pe.wait_ge(yl_ready, 24 + 2 * h)
                else:
                    pe.wait_ge(y_free, 8)
                pe.wait_ge(misc_free, R[f"pt{h}"] + 1)
                if h == 0:
                    for j in range(4):
                        pe.wait_ge(evacuated[j], OUTS["xo"] // 4)
                for vb in range(2):
                    for mt in range(2):
                        c = 256 * h + P * vb
                        last = nc.tensor.matmul(mix[:, 2, 256 * vb:256 * vb + 256], xv[:, mt, c:c + P],
                                                probT[:, h, mt, :], start=mt == 0, stop=mt == 1)
                last.then_inc(y_ready, 1)
            project("xo", yh, yl, T1, (yl_ready, 24))

            def ffn_down(m):
                u0, e0 = UNITS["ffo"][0], OUTS["ffo"]
                pe.wait_ge(evacuated[m % 4], (e0 + m) // 4)
                for k in range(FFN_KB):
                    b = m * FFN_KB + k
                    if b % 8 == 0:
                        pe.wait_ge(lo_ready, u0 + b // 8 + 1)
                    if m == 0:
                        pe.wait_ge(hl_ready, k + 1)
                    last = products(acc[:, m % 4, 0:T1], (u0 + b // 8) % 4, b % 8, hh[:, k, 0:T1], hl[:, k, 0:T1],
                                    k == 0, k == FFN_KB - 1)
                    if b % 8 == 7:
                        last.then_inc(unit_done, 1)

            stream_stats("ffn", T1)
            project("ffi", xh, xl, T1, operand("ffn"))
            for m in range(KB):
                ffn_down(m)

            stream_stats("fin1", T1)
            stream_stats("sb", T2, tiles2)
            project("sq", xh, xl, T2, operand("sb"))
            project("sk", xh, xl, T2)

            at_q, at_c = (0, P, 2 * P), (0, T2, 2 * T2 - P)
            HB = SSD_HEADS + XH

            def sb_scores(h):
                if h >= 4:
                    pe.wait_ge(head_free, HB + h - 3)
                po, b = 64 * (h % 2), h // 2
                pe.wait_ge(evacuated[b % 4], (OUTS["sk"] + b) // 4 + 1)
                for t in range(3):
                    last = nc.tensor.matmul(zbank[h % 4][:, at_c[t]:at_c[t] + T2 - at_q[t]],
                                            skT[po:po + 64, b, P * t:P * t + P], sqT[po:po + 64, b, at_q[t]:T2],
                                            start=t == 0, stop=t == 2)
                last.then_inc(head_ready, 1)

            def sb_after(h):
                z, l = zbank[h % 4], lk[:, h % 2, :]
                pe.wait_ge(lk_step, 2 * h + 2)
                add = dict(start=False, skip_group_check=True)
                nc.tensor.matmul(z[:, 0:T2], tri[:, :], l[:, 0:T2], stop=False, **add)
                nc.tensor.matmul(z[:, P:T2], ones[:, :], l[:, T2:2 * T2 - P], stop=False, **add)
                nc.tensor.matmul(z[:, 2 * P:T2], ones[0:META, :], l[0:META, 2 * T2 - P:ZC], stop=False, **add)
                nc.tensor.matmul(z[:, T2:2 * T2 - P], tri[:, :], l[:, T2:2 * T2 - P], stop=False, **add)
                nc.tensor.matmul(z[:, T2 + P:2 * T2 - P], ones[0:META, :], l[0:META, 2 * T2 - P:ZC], stop=False, **add)
                nc.tensor.matmul(z[:, 2 * T2 - P:ZC], tri[0:META, :], l[0:META, 2 * T2 - P:ZC], stop=True, **add)\
                    .then_inc(tri_ready, 1)

            def sb_out(h):
                po, buf = 64 * (h % 2), h % 2
                dst = obank[h // 2 % 2]
                if h >= 4 and not po:
                    pe.wait_ge(yl_ready, 32 + h // 2 - 1)
                pe.wait_ge(wT_ready, h + 1)
                nc.tensor.matmul(dst[po:po + 64, 0:T2], sv[:, 0, 64 * h:64 * h + 64], wT[:, buf, 0:T2],
                                 start=True, stop=False)
                nc.tensor.matmul(dst[po:po + 64, P:T2], sv[:, 1, 64 * h:64 * h + 64], wT[:, buf, T2:2 * T2 - P],
                                 start=False, stop=False)
                nc.tensor.matmul(dst[po:po + 64, 2 * P:T2], sv[0:META, 2, 64 * h:64 * h + 64],
                                 wT[0:META, buf, 2 * T2 - P:ZC], start=False, stop=True)\
                    .then_inc(pv_done, 1)

            pe.wait_ge(sbmask, 9)
            sb_scores(0)
            sb_scores(1)
            pe.wait_ge(misc_free, R["st_sb"] + 1)
            sb_scores(2)
            for p in range(4):
                token_pair("sv", 2 * p, xh, xl, tiles2)
            for h in range(SBH + 1):
                if h < SBH:
                    sb_after(h)
                if h == 0:
                    for j in range(4):
                        pe.wait_ge(evacuated[j], OUTS["so"] // 4)
                else:
                    sb_out(h - 1)
                if h + 3 < SBH:
                    sb_scores(h + 3)
            project("so", yh, yl, T2, (yl_ready, 32))

            def mlp(n):
                stream_stats(f"mlp{n}", T2)
                project(f"up{n}", xh, xl, T2, operand(f"mlp{n}"))
                with pe.Fori(0, 2) as i:
                    for m in range(4):
                        deep4(f"dn{n}", m, i)

            def deep4(phase, m, i):
                u0, e0 = UNITS[phase][0], OUTS[phase]
                hid0 = FFN_KB + MLP_KB * (phase == "dn1")
                pe.wait_ge(evacuated[m], i + e0 // 4)
                for k in range(MLP_KB):
                    if k % 8 == 0:
                        pe.wait_ge(lo_ready, 16 * i + (u0 + 4 * m + k // 8 + 1))
                    if m == 0:
                        pe.wait_ge(hl_ready, hid0 + k + 1)
                    last = products(acc[:, m, 0:T2], (u0 + k // 8) % 4, k % 8, hh[:, k, :], hl[:, k, :],
                                    k == 0, k == MLP_KB - 1)
                    if k % 8 == 7:
                        last.then_inc(unit_done, 1)

            mlp(0)

            stream_stats("lru", T2)
            project("rec", xh, xl, T2, operand("lru"))
            for gate in range(2):
                u0 = UNITS["rgig"][0] + gate
                pe.wait_ge(lo_ready, u0 + 1)
                for b in range(KB):
                    pe.wait_ge(evacuated[b % 4], OUTS["rgig"] // 4 + (KB * gate + b) // 4)
                    pe.wait_ge(ul_ready, b + 1)
                    last = products(acc[:, b % 4, 0:T2], u0 % 4, b, uh[:, b, :], ul[:, b, :], True, True)
                    last.then_inc(lru_done if b < KB - 1 else unit_done, 1)
            project("gate", xh, xl, T2)
            project("lo", yh, yl, T2, (yl_ready, 40))
            mlp(1)
            stream_stats("fin2", T2)

        @block.scalar
        def _(act):
            def split_hi(base, units=0):
                j = base % 4
                act.wait_ge(landed[j], units * 4 + 16 * (base // 4 + 1))
                if base >= RING:
                    act.wait_ge(unit_done, units + (base - 3))
                act.activation(whi[:, j, :, :].rearrange("p k c -> p (k c)"), raw[:, j, :], ACT.Copy)\
                    .then_inc(hi_ready, 1)

            def square(b, T):
                act.activation(blk(sq, b, 0, T), blk(hT, b, T2 - T, T2), ACT.Square).then_inc(sq_ready, 1)

            def operand(norm, b, T):
                act.activation(blk(xh, b, 0, T), blk(hT, b, T2 - T, T2), ACT.Copy,
                               scale=col(pr, b + PC[norm])).then_inc(xh_ready, 1)
                square(b, T)

            def rms(name, T, tiles=(), norms_before=0):
                act.wait_ge(misc_ready, R["st_" + name] + 1)
                if norms_before:
                    act.wait_ge(rstd_ready, norms_before)
                src = mix[:, MISCB, :]
                ins = act.activation(rt[:, 0:T], src[:, 0:T], ACT.Sqrt, bias=EPS)
                for t, n in enumerate(tiles):
                    ins = act.activation(rtt[0:n, t:t + 1], src[0:n, 300 + t:301 + t], ACT.Sqrt, bias=EPS)
                ins.then_inc(misc_free, 1)

            def exp_ln_tables():
                act.add_instruction(mybir.InstLoadActFuncSet(act_func_set_id=6, name=nc.get_next_instruction_name(),
                                                             engine=mybir.EngineType.Activation))

            def units_loop(phase, body=None):
                u0, n = UNITS[phase]
                with act.Fori(0, n // 4) as i:
                    for j in range(4):
                        split_hi(u0 + j + 4, 4 * i)
                        if body is not None:
                            body(i, j)

            act.dma_start(hT[:, :, META:T2], xT).then_inc(x_in, 16)
            act.dma_start(pr[:, :], par).then_inc(par_in, 16)
            act.dma_start(wsr, wsmall).then_inc(ws_in, 16)
            act.dma_start(wa[32:48, :], wa2).then_inc(wa_in, 16)
            act.dma_start(hT[:, :, 0:META], metaT).then_inc(meta_in, 16)
            for u in range(RING):
                split_hi(u)
            act.wait_ge(x_in, 16)
            act.wait_ge(par_in, 16)
            for b in range(KB):
                operand("mix", b, T1)
            act.wait_ge(ws_in, 16)
            act.activation(wsh[:, :, :].rearrange("p k c -> p (k c)"), wsr, ACT.Copy).then_inc(ws_ready, 1)
            rms("mix", T1, (P, P))

            def softplus_of(x, dst, done, n, **kw):
                act.activation(dst, x, ACT.Abs).then_inc(done, 1)
                act.wait_ge(done, n + 1)
                act.activation(dst, dst, ACT.Exp, scale=-1.0).then_inc(done, 1)
                act.wait_ge(done, n + 2)
                act.activation(dst, dst, ACT.Ln, bias=1.0).then_inc(done, 1)

            last_b = bcn[:, :, :].rearrange("p h (c s) -> p h c s", s=CHUNK)[:, :, :, CHUNK - 1]
            fl = lambda x: x[:, :, :].rearrange("p a b -> p (a b)")
            m = silus = 0
            for phase, count in (("xbc", 12), ("q", 4), ("k", 4), ("v", 8), ("z", 8), ("r", 8), ("gs", 8), ("gg", 8)):
                for n in range(count):
                    if m == 48:
                        act.wait_ge(misc_ready, R["st_ssd"] + 1)
                        act.activation(ry.rearrange("p a b -> p (a b)"), mix[:, MISCB, :], ACT.Sqrt, bias=EPS)\
                            .then_inc(misc_free, 1)
                    if m in (45, 46, 49, 50):
                        h = (45, 46, 49, 50).index(m)
                        act.wait_ge(misc_ready, R[f"o{h}"] + 1)
                        act.activation(o[:, 2 * h:2 * h + 2, :],
                                       mix[:, BANK[f"o{h}"], :].rearrange("p (a b) -> p a b", a=2), ACT.Copy)\
                            .then_inc(misc_free, 1)
                    split_hi(m + 4)
                    dst = dict(z=sz, r=sr, gs=sg1, gg=sg2).get(phase)
                    if dst is not None:
                        act.wait_ge(evacuated[n % 4], (OUTS[phase] + n) // 4 + 1)
                        if phase == "gg":
                            act.wait_ge(n_y, 8)
                        act.activation(dst[:, n, :], t4[:, n % 4, 0:T1], ACT.Tanh).then_inc(th_ready, 1)
                    if m == 1:
                        exp_ln_tables()
                        act.wait_ge(dt_step, 1)
                        softplus_of(xdt[0:16, :], lnb[0:16, :], dt_act, 0)
                        act.activation(expa, pr[0:16, PC["alog"]:PC["alog"] + 1], ACT.Exp).then_inc(dt_act, 1)
                    for c in [c for c in range(12) if SILU_AT[c] == m]:
                        act.wait_ge(conv_step, 4 * c + 5)
                        if c >= 4:
                            act.wait_ge(conv_out, c - 3)
                        act.activation(sg1[:, c % 4, :], xc[:, c, :], ACT.Tanh).then_inc(conv_th, 1)
                    if m == 6:
                        act.wait_ge(misc_free, R["gate1"] + 1)
                        softplus_of(fl(khk), fl(etmp), gla_act, 0)
                    if m == 10:
                        act.wait_ge(gla_step, 2)
                        act.activation(fl(kt), fl(bcn), ACT.Exp, scale=1.0 / 16).then_inc(gla_act, 1)
                    if m == 11:
                        act.wait_ge(gla_step, 3)
                        act.activation(fl(etmp), fl(etmp), ACT.Exp, scale=1.0 / 16).then_inc(gla_act, 1)
                        act.activation(fl(khk), fl(bcn), ACT.Exp, scale=-1.0 / 16).then_inc(gla_act, 1)
                        act.activation(dec, last_b, ACT.Exp, scale=-1.0 / 16).then_inc(gla_act, 1)
                    if m >= 27 and m % 2 and m <= 41:
                        j = (m - 27) // 2
                        for h in (2 * j, 2 * j + 1):
                            act.wait_ge(head_ready, h + 1)
                            if h == 0:
                                act.wait_ge(misc_free, R["ctok"] + 1)
                            if h >= 3:
                                act.wait_ge(y_ready, (h - 3) // 2 + 1)
                            src = mix[:, h % 2, :]
                            act.activation(L[:, h % 3, 0:256], src[:, 0:256], ACT.Exp, scale=-1.0,
                                           bias=ctok[:, 0, h:h + 1])
                            act.activation(L[:, h % 3, 256:384], src[:, 256:384], ACT.Exp, scale=-1.0,
                                           bias=ctok[:, 1, h:h + 1]).then_inc(head_free, 1)
                    if m in (31, 33):
                        t = (m - 31) // 2
                        act.wait_ge(misc_ready, R[f"kht{t}"] + 1)
                        act.activation(khk[:, t, :], mix[:, MISCB, :], ACT.Copy).then_inc(misc_free, 1)
                    if m in (35, 37):
                        t = (m - 35) // 2
                        act.wait_ge(misc_ready, R[f"att{t}"] + 1)
                        act.activation(att[:, t, :, :].rearrange("p h l -> p (h l)"), mix[:, MISCB, :], ACT.Copy)\
                            .then_inc(misc_free, 1)
                    if m in (44, 45):
                        for b in range(4 * (m - 44), 4 * (m - 44) + 4):
                            act.wait_ge(n_y, b + 1)
                            if b == 0:
                                act.wait_ge(y_ready, 8)
                            act.activation(sq[:, b, 0:T1], y[:, b, :], ACT.Square).then_inc(n_sq, 1)
                    if 49 <= m < 57:
                        b = m - 49
                        act.wait_ge(n_y, 9 + b)
                        act.activation(yh[:, b, 0:T1], y[:, b, :], ACT.Copy).then_inc(yh_ready, 1)
                    if m in (50, 51):
                        for h in (2 * (m - 50), 2 * (m - 50) + 1):
                            act.wait_ge(misc_free, R[f"o{h}"] + 1)
                            act.activation(sq[:, 2 * h:2 * h + 2, 0:T1], o[:, 2 * h:2 * h + 2, :], ACT.Square)\
                                .then_inc(n_sq, 1)
                    if m in (53, 55):
                        i = (m - 53) // 2
                        act.wait_ge(misc_ready, R[f"st_gla{i}"] + 1)
                        act.activation(ro[:, 2 * i:2 * i + 2, :],
                                       mix[:, MISCB, :].rearrange("p (a b) -> p a b", a=2), ACT.Sqrt, bias=EPS)\
                            .then_inc(misc_free, 1)
                    m += 1

            act.wait_ge(yl_ready, 8)
            act.dma_start(mem[:, :, :], memT).then_inc(mem_in, 16)
            u0 = UNITS["ups"][0]
            for m in range(8):
                if m == 0:
                    act.wait_ge(unit_done, u0)
                act.wait_ge(n_y, 17 + m)
                act.activation(xh[:, m, 0:T1], o[:, m, :], ACT.Copy).then_inc(yh_ready, 1)
                split_hi(u0 + m + 4)

            def merge(i, j):
                act.wait_ge(merged, 4 * i + (j + 1))
                act.activation(blk(yh, 4 * i + j, 0, T1), blk(sg1, 4 * i + j, 0, T1), ACT.Copy, scale=0.5)\
                    .then_inc(yh_ready, 1)

            units_loop("upg", merge)
            act.wait_ge(mem_in, 16)

            def after_wo(i, j):
                b = 4 * i + j
                act.activation(blk(memh, b, 0, T1), blk(mem, b, 0, T1), ACT.Copy, scale=col(pr, b + PC["mem"]))\
                    .then_inc(memh_ready, 1)
                act.activation(blk(memsq, b, 0, T1), blk(mem, b, 0, T1), ACT.Square).then_inc(memsq_ready, 1)
                act.wait_ge(evacuated[j], i + (OUTS["wo"] // 4 + 1))
                operand("xattn", b, T1)

            units_loop("wo", after_wo)
            rms("mem", T1, (P, P), 1)
            units_loop("xk")
            rms("xattn", T1, (), 2)
            units_loop("xq")
            u0 = UNITS["xv"][0]
            for p in range(XH):
                act.wait_ge(sm_step, 4 * p + 2)
                for t in range(2):
                    ins = act.activation(prob[:, p % 2, t, :], mix[:, p % 2, 256 * t:256 * t + 256], ACT.Exp,
                                         bias=mx[:, p, t:t + 1], accum_out=sums[:, p, t:t + 1])
                ins.then_inc(head_free, 1)
                split_hi(u0 + 2 * p + 4)
                split_hi(u0 + 2 * p + 5)
                act.wait_ge(misc_ready, R[f"pt{p}"] + 1)
                act.activation(probT[:, p, :, :].rearrange("p a b -> p (a b)"), mix[:, MISCB, :], ACT.Copy)\
                    .then_inc(misc_free, 1)
            for h in range(XH):
                act.wait_ge(y_ready, 8 + h + 1)
                for vb in range(2):
                    act.activation(yh[:, 2 * h + vb, 0:T1], mix[:, 2, 256 * vb:256 * vb + 256], ACT.Copy)\
                        .then_inc(yh_ready, 1)

            def after_residual(phase, norm, T):
                def body(i, j):
                    act.wait_ge(evacuated[j], i + (OUTS[phase] // 4 + 1))
                    operand(norm, 4 * i + j, T)
                return body

            units_loop("xo", after_residual("xo", "ffn", T1))

            rms("ffn", T1, (), 3)

            def swiglu(i, j):
                if j % 2 == 0:
                    act.wait_ge(evacuated[j], i + (OUTS["ffi"] // 4 + 1))
                    act.activation(t4[:, j + 1, 0:T1], t4[:, j, 0:T1], ACT.Tanh).then_inc(th_ready, 1)
                else:
                    act.wait_ge(hid_ready, 4 * i + (j + 1))
                    act.activation(blk(hh, 2 * i + j // 2, 0, T1), t4[:, j, 0:T1], ACT.Copy).then_inc(hh_ready, 1)

            units_loop("ffi", swiglu)
            u0, m = UNITS["ffo"][0], 0
            for n in range(22):
                split_hi(u0 + n + 4)
                if (FFN_KB * m + FFN_KB - 1) // 8 == n:
                    act.wait_ge(evacuated[m % 4], (OUTS["ffo"] + m) // 4 + 1)
                    square(m, T1)
                    m += 1
            rms("fin1", T1, (), 4)
            act.wait_ge(meta_in, 16)
            for b in range(KB):
                act.wait_ge(fin_step, b + 1)
                operand("sb", b, T2)
            rms("sb", T2, (P, P, META), 5)

            units_loop("sq")
            units_loop("sk")
            HB = SSD_HEADS + XH
            exp_ln_tables()

            def log_keep(h):
                act.wait_ge(head_ready, HB + h + 1)
                softplus_of(zbank[h % 4][:, 0:ZC], sp[:, h % 4, :], sb_act, 3 * h)

            def pair_out(p):
                act.wait_ge(pv_done, 2 * p + 2)
                act.activation(yh[:, p, :], obank[p % 2][:, 0:T2], ACT.Copy).then_inc(yh_ready, 1)

            log_keep(0)
            log_keep(1)
            log_keep(2)
            u0 = UNITS["sv"][0]
            for m in range(8):
                split_hi(u0 + m + 4)
            for h in range(SBH):
                act.wait_ge(head_free, HB + h + 1)
                act.activation(wT[:, h % 2, :], wT[:, h % 2, :], ACT.Exp).then_inc(wT_ready, 1)
                if h and h % 2 == 0:
                    pair_out(h // 2 - 1)
                if h + 3 < SBH:
                    log_keep(h + 3)
            pair_out(7)
            units_loop("so", after_residual("so", "mlp0", T2))

            def mlp_up(n):
                def body(i, j):
                    act.wait_ge(evacuated[j], i + (OUTS[f"up{n}"] // 4 + 1))
                    act.activation(t4[:, j, :], t4[:, j, :], ACT.Square).then_inc(hid_ready, 1)
                    act.wait_ge(hid_ready, 4 * i + (2 * FFN_KB + MLP_KB * n + j + 1))
                    act.activation(blk(hh, 4 * i + j, 0, T2), t4[:, j, :], ACT.Copy).then_inc(hh_ready, 1)
                return body

            rms("mlp0", T2, (), 6)
            units_loop("up0", mlp_up(0))
            u0 = UNITS["dn0"][0]
            with act.Fori(0, 2) as i:
                for m in range(4):
                    for n in range(4):
                        split_hi(u0 + 4 * m + n + 4, 16 * i)
                    act.wait_ge(evacuated[m], i + (OUTS["dn0"] // 4 + 1))
                    operand("lru", 4 * i + m, T2)

            rms("lru", T2, (), 7)
            act.wait_ge(unit_done, UNITS["rec"][0])
            softplus_of(pr[:, PC["lam"]:PC["lam"] + 8], half[:, 16:24], lam_step, 0)

            def rec(i, j):
                act.wait_ge(lru_step, 16 * i + (4 * j + 4))
                act.activation(blk(uh, 4 * i + j, 0, T2), blk(uu, 4 * i + j, 0, T2), ACT.Copy).then_inc(uh_ready, 1)

            units_loop("rec", rec)
            act.wait_ge(lam_step, 8)
            for gate, (dst, at) in enumerate(((thr, 0), (thi, 8))):
                for b in range(KB):
                    if b < KB - 1:
                        act.wait_ge(lru_done, 7 * gate + b + 1)
                    else:
                        act.wait_ge(unit_done, UNITS["rgig"][0] + gate + 1)
                    act.activation(dst[:, b, :], acc[:, b % 4, 0:T2], ACT.Tanh, scale=0.5,
                                   bias=half[:, at + b:at + b + 1]).then_inc(evacuated[b % 4], 1)
                split_hi(UNITS["rgig"][0] + gate + 4)
            act.wait_ge(lru_step, 33)
            act.activation(fl(thr), fl(aa), ACT.Tanh).then_inc(lru_act, 1)
            act.activation(fl(aa), fl(aa), ACT.Exp).then_inc(lru_act, 1)
            u0 = UNITS["gate"][0]
            for m in range(8):
                split_hi(u0 + m + 4)
                if m == 2:
                    act.wait_ge(lru_step, 35)
                    ra = recin[:, :, :].rearrange("p a b -> p (a b)")[:, 0:KB * T2]
                    act.activation(ra, ra, ACT.Sqrt, scale=-0.25).then_inc(lru_act, 1)
            for b in range(KB):
                act.wait_ge(evacuated[b % 4], (OUTS["gate"] + b) // 4 + 1)
                act.activation(gg[:, b, :], gg[:, b, :], ACT.Gelu_apprx_tanh).then_inc(th_ready, 1)
            for b in range(KB):
                act.wait_ge(merged, 8 + b + 1)
                act.activation(yh[:, b, :], gg[:, b, :], ACT.Copy).then_inc(yh_ready, 1)
            units_loop("lo", after_residual("lo", "mlp1", T2))
            rms("mlp1", T2, (), 8)
            units_loop("up1", mlp_up(1))
            u0 = UNITS["dn1"][0]
            for m in range(8):
                for n in range(4):
                    if u0 + 4 * m + n + 4 < NU:
                        split_hi(u0 + 4 * m + n + 4)
                act.wait_ge(evacuated[m % 4], (OUTS["dn1"] + m) // 4 + 1)
                square(m, T2)
            rms("fin2", T2, (), 9)

        @block.vector
        def _(dve):
            def split_lo(base, units=0):
                j = base % 4
                dve.wait_ge(hi_ready, units + (base + 1))
                dve.tensor_tensor(wlo[:, j, :, :].rearrange("p k c -> p (k c)"), raw[:, j, :],
                                  whi[:, j, :, :].rearrange("p k c -> p (k c)").bitcast(F32), ALU.subtract)\
                    .then_inc(lo_ready, 1)

            def operand_lo(norm, b, T, n):
                dve.wait_ge(xh_ready, n + 1)
                dve.scalar_tensor_tensor(out=blk(xl, b, 0, T), in0=blk(hT, b, T2 - T, T2), scalar=col(pr, b + PC[norm]),
                                         in1=blk(xh, b, 0, T).bitcast(F32), op0=ALU.mult, op1=ALU.subtract)\
                    .then_inc(xl_ready, 1)

            def units_loop(phase, body, after=None):
                u0, n = UNITS[phase]
                with dve.Fori(0, n // 4) as i:
                    for j in range(4):
                        dve.wait_ge(unit_done, 4 * i + (u0 + j + 1))
                        body(i, j)
                        split_lo(u0 + j + 4, 4 * i)
                        if after is not None:
                            after(i, j)

            norms = [0]

            def inverse_rms(name, T, tiles=(), dst=None, halved=False):
                dve.wait_ge(misc_free, R["st_" + name] + 1)
                dst = rstd if dst is None else dst
                for t, n in enumerate(tiles):
                    dve.reciprocal(rtok[0:n, t:t + 1], rtt[0:n, t:t + 1])
                dve.reciprocal(dst[:, 0:T], rt[:, 0:T]).then_inc(rstd_ready, 1)
                norms[0] += 1
                dve.wait_ge(rstd_ready, norms[0])
                if halved:
                    dve.tensor_scalar(rstdh[:, 0:T], dst[:, 0:T], 0.5, None, ALU.mult).then_inc(rstdh_ready, 1)

            def residual(phase, norm, T):
                def body(i, j):
                    h = blk(hT, 4 * i + j, T2 - T, T2)
                    dve.tensor_tensor(h, acc[:, j, 0:T], h, ALU.add).then_inc(evacuated[j], 1)

                def after(i, j):
                    operand_lo(norm, 4 * i + j, T, 4 * i + (KB * OPER[norm] + j))
                return body, after

            def scaled(dst, T, by=None, times=None):
                def body(i, j):
                    d = blk(dst, 4 * i + j, 0, T)
                    r = (rstd if by is None else by)[:, 0:T]
                    if times is None:
                        ins = dve.tensor_tensor(d, acc[:, j, 0:T], r, ALU.mult)
                    else:
                        ins = dve.scalar_tensor_tensor(out=d, in0=acc[:, j, 0:T], scalar=times, in1=r,
                                                       op0=ALU.mult, op1=ALU.mult)
                    ins.then_inc(evacuated[j], 1)
                return body

            def token_scaled(dst, m, tiles):
                c = 128 * m
                if len(tiles) == 3:
                    dve.tensor_scalar(dst[0:META, 2, c:c + 256], acc[0:META, m % 4, 256:512], rtok[0:META, 2:3], None,
                                      ALU.mult)
                for t in range(2):
                    dve.tensor_scalar(dst[:, t, c:c + 256], acc[:, m % 4 + t, 0:256], rtok[:, t:t + 1], None, ALU.mult)\
                        .then_inc(evacuated[m % 4 + t], 1)

            for u in range(RING):
                split_lo(u)
            dve.wait_ge(par_in, 16)
            dve.wait_ge(x_in, 16)
            dve.tensor_scalar(halfc, pr[:, PC["convw"]:PC["convw"] + 60], 0.5, None, ALU.mult).then_inc(conv_step, 1)
            for b in range(KB):
                operand_lo("mix", b, T1, b)
            dve.wait_ge(ws_ready, 1)
            dve.tensor_tensor(wsl[:, :, :].rearrange("p k c -> p (k c)"), wsr,
                              wsh[:, :, :].rearrange("p k c -> p (k c)").bitcast(F32), ALU.subtract)\
                .then_inc(wsl_ready, 1)
            inverse_rms("mix", T1, (P, P), halved=True)
            dve.wait_ge(rstdh_ready, 1)
            dve.wait_ge(consts, 16)
            fl = lambda x: x[:, :, :].rearrange("p a b -> p (a b)")
            gx = fl(khk).rearrange("p (h t) -> p h t", h=4)
            misc = mix[:, MISCB, :]

            def gla_norm(b):
                dve.wait_ge(n_r, 2 + b // 4)
                dve.scalar_tensor_tensor(out=o[:, b, :], in0=o[:, b, :], scalar=g("glan", b % 2), in1=ro[:, b // 2, :],
                                         op0=ALU.mult, op1=ALU.mult).then_inc(o_step, 1)
                dve.wait_ge(o_step, b + 1)
                dve.wait_ge(silu_done, 16)
                dve.tensor_tensor(o[:, b, :], o[:, b, :], sr[:, b, :], ALU.mult).then_inc(n_y, 1)

            m = silus = 0
            for phase, count in (("xbc", 12), ("q", 4), ("k", 4), ("v", 8), ("z", 8), ("r", 8), ("gs", 8), ("gg", 8)):
                for n in range(count):
                    j = n % 4
                    if m == 0:
                        dve.wait_ge(misc_ready, R["small"] + 1)
                        dve.tensor_tensor(smt[0:48, :], misc[0:48, 0:T1], rstd[0:48, 0:T1], ALU.mult)\
                            .then_inc(misc_free, 1)
                        dve.wait_ge(misc_free, R["small"] + 1)
                        dve.tensor_scalar(xdt[0:16, :], smt[0:16, :], g("dtb")[0:16, :], None, ALU.add)\
                            .then_inc(dt_step, 1)
                    if 39 <= m < 45:
                        c, hp = divmod(m - 39, 2)
                        dve.wait_ge(misc_ready, R[f"u{m - 39}"] + 1)
                        for h in (2 * hp, 2 * hp + 1):
                            u = misc[:, 256 * (h % 2):256 * (h % 2) + 256]
                            if c == 0:
                                ins = dve.tensor_copy(state[0][:, h, :], u)
                            else:
                                dve.wait_ge(misc_free, R[f"u{2 * (c - 1) + hp}"] + 1)
                                ins = dve.scalar_tensor_tensor(out=state[c][:, h, :], in0=state[c - 1][:, h, :],
                                                               scalar=dec[:, h, c:c + 1], in1=u,
                                                               op0=ALU.mult, op1=ALU.add)
                        ins.then_inc(misc_free, 1)
                    dve.wait_ge(unit_done, m + 1 if phase != "v" else m + 1 + (1 - n % 2))
                    if phase == "xbc":
                        dve.tensor_tensor(convin[:, n, 3:3 + T1], acc[:, j, 0:T1], rstd[:, 0:T1], ALU.mult)\
                            .then_inc(evacuated[j], 1)
                    elif phase in ("q", "k"):
                        dve.tensor_tensor((qf if phase == "q" else kf)[:, n, :], acc[:, j, 0:T1], rstd[:, 0:T1],
                                          ALU.mult).then_inc(evacuated[j], 1)
                    elif phase == "v":
                        if n % 2:
                            token_scaled(vt, n - 1, (P, P))
                    else:
                        if silus >= 4:
                            dve.wait_ge(th_ready, silus - 3)
                        dve.tensor_tensor(t4[:, j, 0:T1], acc[:, j, 0:T1], rstdh[:, 0:T1], ALU.mult)\
                            .then_inc(evacuated[j], 1)
                    split_lo(m + 4)
                    if phase in ("z", "r"):
                        s = (sz if phase == "z" else sr)[:, n, :]
                        dve.wait_ge(th_ready, silus + 1)
                        dve.scalar_tensor_tensor(out=s, in0=s, scalar=1.0, in1=t4[:, j, 0:T1], op0=ALU.add, op1=ALU.mult)\
                            .then_inc(silu_done, 1)
                    if phase in ("z", "r", "gs", "gg"):
                        silus += 1
                    if m == 3:
                        dve.wait_ge(dt_act, 4)
                        dve.scalar_tensor_tensor(out=dtT[0:16, :], in0=xdt[0:16, :], scalar=0.0, in1=lnb[0:16, :],
                                                 op0=ALU.max, op1=ALU.add).then_inc(dt_step, 1)
                        dve.wait_ge(dt_step, 2)
                        dve.tensor_scalar(adt[0:16, :], dtT[0:16, :], expa, None, ALU.mult).then_inc(dt_step, 1)
                        dve.wait_ge(dt_step, 3)
                        dve.tensor_tensor_scan(csn[:, 0:T1], one16[0:16, :], adt[0:16, :], 0.0, ALU.mult, ALU.add)\
                            .then_inc(dt_step, 1)
                        dve.wait_ge(dt_step, 4)
                        dve.tensor_copy(csn[:, T1:384], csn[:, P:T1]).then_inc(dt_step, 1)
                    if m == 4:
                        for i in range(4):
                            dve.wait_ge(misc_ready, R[f"gate{i // 2}"] + 1)
                            ins = dve.tensor_scalar(gx[:, i, :], mix[:, BANK[f"gate{i // 2}"], 256 * (i % 2):256 * (i % 2) + 256],
                                                    g("glab", i), -1.0, ALU.add, ALU.mult)
                            if i % 2:
                                ins.then_inc(misc_free, 1)
                    if m == 8:
                        dve.wait_ge(gla_act, 3)
                        dve.scalar_tensor_tensor(out=fl(khk), in0=fl(khk), scalar=0.0, in1=fl(etmp),
                                                 op0=ALU.max, op1=ALU.add).then_inc(gla_step, 1)
                        dve.wait_ge(gla_step, 1)
                        dve.tensor_tensor_scan(fl(bcn), fl(kt), fl(khk), 0.0, ALU.mult, ALU.add).then_inc(gla_step, 1)
                    if m == 9:
                        dve.wait_ge(gla_step, 2)
                        bc = bcn[:, :, :].rearrange("p h (c s) -> p (h c) s", s=CHUNK)
                        dve.tensor_tensor(etmp[:, :, :].rearrange("p h (c s) -> p (h c) s", s=CHUNK), bc,
                                          bc[:, :, CHUNK - 1:CHUNK].broadcast_to([P, 16, CHUNK]), ALU.subtract)\
                            .then_inc(gla_step, 1)
                    if m == 6:
                        dve.wait_ge(misc_ready, R["ctok"] + 1)
                        dve.tensor_copy(ctok[:, :, :].rearrange("p a b -> p (a b)"), misc[:, 0:64]).then_inc(misc_free, 1)
                    for c in [c for c in range(12) if CONV_AT[c] == m]:
                        x = convin[:, c, :]
                        if c == 0:
                            dve.wait_ge(conv_step, 1)
                        dve.wait_ge(evacuated[c % 4], c // 4 + 1)
                        dve.tensor_scalar(xc[:, c, :], x[:, 3:3 + T1], halfc[:, 36 + c:37 + c], halfc[:, 48 + c:49 + c],
                                          ALU.mult, ALU.add).then_inc(conv_step, 1)
                        for tap in (2, 1, 0):
                            dve.wait_ge(conv_step, 4 * c + 4 - tap)
                            dve.scalar_tensor_tensor(out=xc[:, c, :], in0=x[:, tap:tap + T1],
                                                     scalar=halfc[:, 12 * tap + c:12 * tap + c + 1], in1=xc[:, c, :],
                                                     op0=ALU.mult, op1=ALU.add).then_inc(conv_step, 1)
                    for c in [c for c in range(12) if SILU_AT[c] == m - 1]:
                        dve.wait_ge(conv_th, c + 1)
                        dve.scalar_tensor_tensor(out=xc[:, c, :], in0=sg1[:, c % 4, :], scalar=1.0, in1=xc[:, c, :],
                                                 op0=ALU.add, op1=ALU.mult).then_inc(conv_out, 1)
                    if m == 22:
                        dve.wait_ge(gla_act, 7)
                        for i in range(4):
                            dve.wait_ge(evacuated[i], OUTS["v"] // 4)
                        dve.tensor_tensor(fl(etmp), fl(kf), fl(etmp), ALU.mult).then_inc(gla_step, 1)
                    if m == 24:
                        dve.tensor_tensor(fl(kt), fl(kf), fl(kt), ALU.mult).then_inc(gla_step, 1)
                    if m == 26:
                        dve.scalar_tensor_tensor(out=fl(qf), in0=fl(qf), scalar=float(P) ** -0.5, in1=fl(khk),
                                                 op0=ALU.mult, op1=ALU.mult).then_inc(gla_step, 1)
                    if m == 21:
                        for grp in range(2):
                            dve.wait_ge(misc_ready, R[f"cb{grp}"] + 1)
                            dve.tensor_copy(CB[:, grp, :], mix[:, BANK[f"cb{grp}"], 0:384]).then_inc(misc_free, 1)
                    if m in (21, 23):
                        for i in (m - 21, m - 20):
                            t, hf = divmod(i, 2)
                            dve.wait_ge(misc_ready, R[f"xt{i}"] + 1)
                            dve.tensor_tensor(xk_[:, t, 512 * hf:512 * hf + 512].rearrange("p (h c) -> p h c", c=64),
                                              mix[:, BANK[f"xt{i}"], :].rearrange("p (h c) -> p h c", c=64),
                                              ctok[:, 2 + t, 8 * hf:8 * hf + 8].rearrange("p (h o) -> p h o", o=1)
                                              .broadcast_to([P, 8, 64]), ALU.mult).then_inc(misc_free, 1)
                    if m >= 27 and m % 2 and m <= 43:
                        j = (m - 27) // 2
                        if j:
                            b = j - 1
                            dve.wait_ge(y_ready, b + 1)
                            dve.scalar_tensor_tensor(out=y[:, b, :], in0=xc[:, b, :], scalar=g("dskip", b),
                                                     in1=mix[:, 2, 0:T1], op0=ALU.mult, op1=ALU.add)\
                                .then_inc(y_free, 1)
                            dve.wait_ge(y_free, b + 1)
                            dve.wait_ge(silu_done, b + 1)
                            dve.tensor_tensor(y[:, b, :], y[:, b, :], sz[:, b, :], ALU.mult).then_inc(n_y, 1)
                    if m == 48:
                        dve.wait_ge(misc_free, R["st_ssd"] + 1)
                        ryf = ry.rearrange("p a b -> p (a b)")
                        dve.reciprocal(ryf, ryf).then_inc(n_r, 1)
                        dve.wait_ge(n_r, 1)
                    if 48 <= m < 56:
                        b = m - 48
                        dve.wait_ge(n_sq, 8)
                        dve.scalar_tensor_tensor(out=y[:, b, :], in0=y[:, b, :], scalar=g("ssdn", b),
                                                 in1=ry[:, b // 4, :], op0=ALU.mult, op1=ALU.mult).then_inc(n_y, 1)
                    if m in (54, 56):
                        i = (m - 54) // 2
                        dve.wait_ge(misc_free, R[f"st_gla{i}"] + 1)
                        r = ro[:, 2 * i:2 * i + 2, :].rearrange("p a b -> p (a b)")
                        dve.reciprocal(r, r).then_inc(n_r, 1)
                    if m in (57, 58, 59):
                        for b in ((0, 1), (2, 3), (4, 5))[m - 57]:
                            gla_norm(b)
                    m += 1

            u0 = UNITS["ups"][0]
            dve.wait_ge(th_ready, 32)
            dve.wait_ge(yl_ready, 8)
            for m in range(8):
                if m < 2:
                    gla_norm(6 + m)
                dve.wait_ge(unit_done, u0 + m + 1)
                dve.scalar_tensor_tensor(out=sg1[:, m, :], in0=sg1[:, m, :], scalar=1.0, in1=acc[:, m % 4, 0:T1],
                                         op0=ALU.add, op1=ALU.mult).then_inc(evacuated[m % 4], 1)
                dve.wait_ge(yh_ready, 8 + m + 1)
                dve.tensor_tensor(xl[:, m, 0:T1], o[:, m, :], xh[:, m, 0:T1].bitcast(F32), ALU.subtract)\
                    .then_inc(yl_ready, 1)
                split_lo(u0 + m + 4)

            def merge(i, j):
                b = 4 * i + j
                dve.scalar_tensor_tensor(out=t4[:, j, 0:T1], in0=blk(sg2, b, 0, T1), scalar=1.0, in1=acc[:, j, 0:T1],
                                         op0=ALU.add, op1=ALU.mult).then_inc(evacuated[j], 1)
                dve.wait_ge(evacuated[j], i + (OUTS["upg"] // 4 + 1))
                s = blk(sg1, b, 0, T1)
                dve.tensor_tensor(s, s, t4[:, j, 0:T1], ALU.add).then_inc(merged, 1)

            def merge_lo(i, j):
                b = 4 * i + j
                dve.wait_ge(yh_ready, 4 * i + (16 + j + 1))
                dve.scalar_tensor_tensor(out=blk(yl, b, 0, T1), in0=blk(sg1, b, 0, T1), scalar=0.5,
                                         in1=blk(yh, b, 0, T1).bitcast(F32), op0=ALU.mult, op1=ALU.subtract)\
                    .then_inc(yl_ready, 1)

            units_loop("upg", merge, merge_lo)
            body, after = residual("wo", "xattn", T1)

            def mem_lo(i, j):
                b = 4 * i + j
                dve.wait_ge(memh_ready, b + 1)
                dve.scalar_tensor_tensor(out=blk(meml, b, 0, T1), in0=blk(mem, b, 0, T1), scalar=col(pr, b + PC["mem"]),
                                         in1=blk(memh, b, 0, T1).bitcast(F32), op0=ALU.mult, op1=ALU.subtract)\
                    .then_inc(meml_ready, 1)
                after(i, j)

            units_loop("wo", body, mem_lo)
            inverse_rms("mem", T1, (P, P), dst=rstdm)
            units_loop("xk", scaled(xkT, T1, by=rstdm))
            inverse_rms("xattn", T1)
            units_loop("xq", scaled(xqT, T1, times=1.0 / 16))
            u0 = UNITS["xv"][0]
            for p in range(XH):
                dve.wait_ge(head_ready, SSD_HEADS + p + 1)
                dve.reduce_max(mx[:, p, :], mix[:, p % 2, :].rearrange("p (t k) -> p t k", t=2), AX).then_inc(sm_step, 1)
                dve.wait_ge(sm_step, 4 * p + 1)
                dve.tensor_scalar(mx[:, p, :], mx[:, p, :], -1.0, None, ALU.mult).then_inc(sm_step, 1)
                dve.wait_ge(head_free, SSD_HEADS + p + 1)
                dve.reciprocal(rsum[:, p, :], sums[:, p, :]).then_inc(sm_step, 1)
                dve.wait_ge(sm_step, 4 * p + 3)
                dve.tensor_tensor(prob[:, p % 2, :, :], prob[:, p % 2, :, :],
                                  rsum[:, p, :].rearrange("p (t o) -> p t o", o=1).broadcast_to([P, 2, T1]), ALU.mult)\
                    .then_inc(sm_step, 1)
                dve.wait_ge(unit_done, u0 + 2 * p + 2)
                token_scaled(xv, 2 * p, (P, P))
                split_lo(u0 + 2 * p + 4)
                split_lo(u0 + 2 * p + 5)
            for h in range(XH):
                for vb in range(2):
                    dve.wait_ge(yh_ready, 24 + 2 * h + 2)
                    dve.tensor_tensor(yl[:, 2 * h + vb, 0:T1], mix[:, 2, 256 * vb:256 * vb + 256],
                                      yh[:, 2 * h + vb, 0:T1].bitcast(F32), ALU.subtract).then_inc(yl_ready, 1)
            units_loop("xo", *residual("xo", "ffn", T1))

            inverse_rms("ffn", T1, halved=True)
            dve.wait_ge(rstdh_ready, 2)

            def swiglu(i, j):
                if j % 2 == 0:
                    dve.tensor_tensor(t4[:, j, 0:T1], acc[:, j, 0:T1], rstdh[:, 0:T1], ALU.mult)\
                        .then_inc(evacuated[j], 1)
                else:
                    g_, u_ = t4[:, j - 1, 0:T1], t4[:, j, 0:T1]
                    dve.wait_ge(th_ready, 2 * i + (32 + j // 2 + 1))
                    dve.scalar_tensor_tensor(out=g_, in0=u_, scalar=1.0, in1=g_, op0=ALU.add, op1=ALU.mult)\
                        .then_inc(hid_ready, 1)
                    dve.wait_ge(hid_ready, 4 * i + j)
                    dve.tensor_tensor(u_, acc[:, j, 0:T1], g_, ALU.mult).then_inc(evacuated[j], 1)
                    dve.wait_ge(evacuated[j], i + (OUTS["ffi"] // 4 + 1))
                    dve.tensor_tensor(u_, u_, rstd[:, 0:T1], ALU.mult).then_inc(hid_ready, 1)

            def swiglu_lo(i, j):
                if j % 2:
                    b = 2 * i + j // 2
                    dve.wait_ge(hh_ready, b + 1)
                    dve.tensor_tensor(blk(hl, b, 0, T1), t4[:, j, 0:T1], blk(hh, b, 0, T1).bitcast(F32), ALU.subtract)\
                        .then_inc(hl_ready, 1)

            units_loop("ffi", swiglu, swiglu_lo)
            u0, m = UNITS["ffo"][0], 0
            for n in range(22):
                dve.wait_ge(unit_done, u0 + n + 1)
                if (FFN_KB * m + FFN_KB - 1) // 8 == n:
                    h = hT[:, m, META:T2]
                    dve.tensor_tensor(h, acc[:, m % 4, 0:T1], h, ALU.add).then_inc(evacuated[m % 4], 1)
                    m += 1
                split_lo(u0 + n + 4)

            def final(name, T):
                inverse_rms(name, T)
                for j in range(4):
                    dve.wait_ge(evacuated[j], OUTS["sq"] // 4)
                for b in range(KB):
                    h = hT[:, b, T2 - T:T2]
                    dve.scalar_tensor_tensor(out=h, in0=h, scalar=g(name, b), in1=rstd[:, 0:T], op0=ALU.mult,
                                             op1=ALU.mult).then_inc(fin_step, 1)

            final("fin1", T1)
            dve.wait_ge(fin_step, KB)
            for b in range(KB):
                operand_lo("sb", b, T2, KB * OPER["sb"] + b)
            inverse_rms("sb", T2, (P, P, META))

            units_loop("sq", scaled(sqT, T2, times=0.125))
            units_loop("sk", scaled(skT, T2))
            HB = SSD_HEADS + XH
            dve.wait_ge(sbmask, 9)

            def log_keep(h):
                s = sp[:, h % 4, :]
                dve.wait_ge(sb_act, 3 * h + 3)
                dve.scalar_tensor_tensor(out=s, in0=zbank[h % 4][:, 0:ZC], scalar=0.0, in1=s, op0=ALU.max, op1=ALU.add)\
                    .then_inc(lk_step, 1)
                dve.wait_ge(lk_step, 2 * h + 1)
                if h >= 2:
                    dve.wait_ge(tri_ready, h - 1)
                dve.tensor_tensor(lk[:, h % 2, :], s, nmask[:, :], ALU.mult).then_inc(lk_step, 1)

            def pair_lo(p):
                dve.wait_ge(yh_ready, 32 + p + 1)
                dve.tensor_tensor(yl[:, p, :], obank[p % 2][:, 0:T2], yh[:, p, :].bitcast(F32), ALU.subtract)\
                    .then_inc(yl_ready, 1)

            log_keep(0)
            log_keep(1)
            u0 = UNITS["sv"][0]
            for p in range(4):
                dve.wait_ge(unit_done, u0 + 2 * p + 2)
                token_scaled(sv, 2 * p, (P, P, META))
                split_lo(u0 + 2 * p + 4)
                split_lo(u0 + 2 * p + 5)
            for h in range(SBH):
                dve.wait_ge(tri_ready, h + 1)
                if h >= 2:
                    dve.wait_ge(pv_done, h - 1)
                dve.scalar_tensor_tensor(out=wT[:, h % 2, :], in0=zbank[h % 4][:, 0:ZC], scalar=0.0, in1=bmask[:, :],
                                         op0=ALU.min, op1=ALU.add).then_inc(head_free, 1)
                if h + 2 < SBH:
                    log_keep(h + 2)
                if h and h % 2 == 0:
                    pair_lo(h // 2 - 1)
            pair_lo(7)
            units_loop("so", *residual("so", "mlp0", T2))

            def mlp_up(n):
                def body(i, j):
                    dve.scalar_tensor_tensor(out=t4[:, j, :], in0=acc[:, j, 0:T2], scalar=0.0, in1=rstd[:, :],
                                             op0=ALU.max, op1=ALU.mult).then_inc(evacuated[j], 1)

                def lo_part(i, j):
                    b = 4 * i + j
                    dve.wait_ge(hh_ready, 4 * i + (FFN_KB + MLP_KB * n + j + 1))
                    dve.tensor_tensor(blk(hl, b, 0, T2), t4[:, j, :], blk(hh, b, 0, T2).bitcast(F32), ALU.subtract)\
                        .then_inc(hl_ready, 1)

                def lagged(i, j):
                    body(i, j)
                    if j:
                        lo_part(i, j - 1)

                return lagged, lambda i, j: lo_part(i, j) if j == 3 else None

            inverse_rms("mlp0", T2)
            units_loop("up0", *mlp_up(0))
            u0 = UNITS["dn0"][0]
            with dve.Fori(0, 2) as i:
                for m in range(4):
                    for n in range(4):
                        dve.wait_ge(unit_done, 16 * i + (u0 + 4 * m + n + 1))
                        if n == 3:
                            h = blk(hT, 4 * i + m, 0, T2)
                            dve.tensor_tensor(h, acc[:, m, 0:T2], h, ALU.add).then_inc(evacuated[m], 1)
                        split_lo(u0 + 4 * m + n + 4, 16 * i)
                    operand_lo("lru", 4 * i + m, T2, 4 * i + (KB * OPER["lru"] + m))

            inverse_rms("lru", T2)
            dve.wait_ge(lru_zero, 1)
            dve.wait_ge(lam_step, 3)
            lam, soft, negc = pr[:, PC["lam"]:PC["lam"] + 8], half[:, 16:24], half[:, 24:32]
            dve.tensor_scalar(negc, lam, -1.0, 0.0, ALU.mult, ALU.max).then_inc(lam_step, 1)
            dve.wait_ge(lam_step, 4)
            dve.tensor_tensor(soft, negc, soft, ALU.add).then_inc(lam_step, 1)
            dve.wait_ge(lam_step, 5)
            dve.tensor_scalar(negc, soft, -4.0, None, ALU.mult).then_inc(lam_step, 1)
            for n in range(2):
                dve.tensor_scalar(half[:, 8 * n:8 * n + 8], pr[:, PC["brg"] + 8 * n:PC["brg"] + 8 * n + 8], 0.5, None,
                                  ALU.mult).then_inc(lam_step, 1)

            def rec_conv(i, j):
                b = 4 * i + j
                u_ = blk(uu, b, 0, T2)
                dve.wait_ge(evacuated[j], i + (OUTS["rec"] // 4 + 1))
                dve.tensor_scalar(u_, blk(recin, b, 3, 3 + T2), col(pr, b + (PC["lconvw"] + 24)),
                                  col(pr, b + PC["lconvb"]), ALU.mult, ALU.add).then_inc(lru_step, 1)
                for tap in (2, 1, 0):
                    dve.wait_ge(lru_step, 16 * i + (4 * j + 3 - tap))
                    dve.scalar_tensor_tensor(out=u_, in0=blk(recin, b, tap, tap + T2),
                                             scalar=col(pr, b + (PC["lconvw"] + 8 * tap)), in1=u_,
                                             op0=ALU.mult, op1=ALU.add).then_inc(lru_step, 1)
                dve.wait_ge(uh_ready, 4 * i + (j + 1))
                dve.tensor_tensor(blk(ul, b, 0, T2), u_, blk(uh, b, 0, T2).bitcast(F32), ALU.subtract)\
                    .then_inc(ul_ready, 1)

            def rec(i, j):
                dve.tensor_tensor(blk(recin, 4 * i + j, 3, 3 + T2), acc[:, j, 0:T2], rstd[:, :], ALU.mult)\
                    .then_inc(evacuated[j], 1)

            units_loop("rec", rec, rec_conv)
            for gate in range(2):
                dve.wait_ge(unit_done, UNITS["rgig"][0] + gate + 1)
                split_lo(UNITS["rgig"][0] + gate + 4)
            for j in range(4):
                dve.wait_ge(evacuated[j], OUTS["gate"] // 4)
            dve.wait_ge(lam_step, 8)
            for b in range(KB):
                ins = dve.tensor_scalar(aa[:, b, :], thr[:, b, :], 1.0, negc[:, b:b + 1], ALU.add, ALU.mult)
            ins.then_inc(lru_step, 1)
            ra = recin[:, :, :].rearrange("p a b -> p (a b)")[:, 0:KB * T2]
            u0 = UNITS["gate"][0]
            for m in range(8):
                dve.wait_ge(unit_done, u0 + m + 1)
                dve.tensor_tensor(gg[:, m, :], acc[:, m % 4, 0:T2], rstd[:, :], ALU.mult).then_inc(evacuated[m % 4], 1)
                split_lo(u0 + m + 4)
                if m == 0:
                    dve.wait_ge(lru_act, 2)
                    dve.tensor_tensor(ra, fl(aa), fl(aa), ALU.mult).then_inc(lru_step, 1)
                    dve.wait_ge(lru_step, 34)
                    dve.scalar_tensor_tensor(out=ra, in0=ra, scalar=1.0, in1=fl(thr), op0=ALU.add, op1=ALU.mult)\
                        .then_inc(lru_step, 1)
                if m == 1:
                    dve.scalar_tensor_tensor(out=fl(thi), in0=fl(thi), scalar=1.0, in1=fl(uu), op0=ALU.add,
                                             op1=ALU.mult).then_inc(lru_step, 1)
                if m == 3:
                    dve.wait_ge(lru_act, 3)
                    dve.wait_ge(lru_step, 36)
                    dve.tensor_tensor(fl(thi), fl(thi), ra, ALU.mult).then_inc(lru_step, 1)
                if m == 4:
                    dve.wait_ge(lru_step, 37)
                    for b in range(KB):
                        dve.tensor_tensor_scan(uu[:, b, :], aa[:, b, :], thi[:, b, :], 0.0, ALU.mult, ALU.add)\
                            .then_inc(lru_step, 1)
            dve.wait_ge(lru_step, 45)
            for b in range(KB):
                dve.wait_ge(th_ready, 32 + FFN_KB + b + 1)
                dve.tensor_tensor(gg[:, b, :], uu[:, b, :], gg[:, b, :], ALU.mult).then_inc(merged, 1)
            for b in range(KB):
                dve.wait_ge(yh_ready, 40 + b + 1)
                dve.tensor_tensor(yl[:, b, :], gg[:, b, :], yh[:, b, :].bitcast(F32), ALU.subtract)\
                    .then_inc(yl_ready, 1)
            units_loop("lo", *residual("lo", "mlp1", T2))
            inverse_rms("mlp1", T2)
            units_loop("up1", *mlp_up(1))
            u0 = UNITS["dn1"][0]
            for m in range(8):
                for n in range(4):
                    dve.wait_ge(unit_done, u0 + 4 * m + n + 1)
                    if n == 3:
                        dve.tensor_tensor(hT[:, m, :], acc[:, m % 4, 0:T2], hT[:, m, :], ALU.add)\
                            .then_inc(evacuated[m % 4], 1)
                    if u0 + 4 * m + n + 4 < NU:
                        split_lo(u0 + 4 * m + n + 4)
            final("fin2", T2)


def stream(i):
    import numpy as np
    w = i["w_in"][0]
    cut = np.cumsum([0, 1024, 1536, 16, 512, 512, 1024, 1024, 16, 1024, 1024])
    z, xbc, dt, q, k, v, r, a1, gs, gg = [w[:, cut[n]:cut[n + 1]] for n in range(10)]

    def cols(a):
        return a.reshape(8, 128, -1, 128).transpose(2, 1, 0, 3).reshape(-1, 128, 1024)

    def deep(a):
        b = a.reshape(-1, 128, 8, 128).transpose(2, 0, 1, 3).reshape(-1, 8, 128, 128)
        return b.transpose(0, 2, 1, 3).reshape(-1, 128, 1024)

    kv, fi, qkv, li = i["w_xkv"][0], i["w_ffn_in"][0], i["sb_w_qkv_2"][0], i["lru_w_in_2"][0]
    g, u = cols(fi[:, :2816]), cols(fi[:, 2816:])
    gates = [i[n][0].transpose(1, 0, 2).reshape(1, 128, 1024) for n in ("lru_w_rg_2", "lru_w_ig_2")]
    parts = {
        "xbc": cols(xbc), "q": cols(q), "k": cols(k), "v": cols(v), "z": cols(z), "r": cols(r),
        "gs": cols(gs), "gg": cols(gg), "ups": cols(i["w_up_ssd"][0]), "upg": cols(i["w_up_gla"][0]),
        "wo": cols(i["w_o"][0]), "xk": cols(kv[:, :1024]), "xq": cols(i["w_xq"][0]),
        "xv": cols(kv[:, 1024:]), "xo": cols(i["w_xo"][0]),
        "ffi": np.stack([g, u], 1).reshape(44, 128, 1024), "ffo": deep(i["w_ffn_out"][0]),
        "sq": cols(qkv[:, :1024]), "sk": cols(qkv[:, 1024:2048]), "sv": cols(qkv[:, 2048:]),
        "so": cols(i["sb_w_o_2"][0]), "up0": cols(i["mlp_w_up_2"][0]), "dn0": deep(i["mlp_w_down_2"][0]),
        "rec": cols(li[:, 1024:]), "rgig": np.concatenate(gates), "gate": cols(li[:, :1024]),
        "lo": cols(i["lru_w_out_2"][0]), "up1": cols(i["mlp_w_up_2"][1]), "dn1": deep(i["mlp_w_down_2"][1]),
    }
    for name, n, _ in PHASES:
        assert parts[name].shape == (n, 128, 1024), name
    small = np.zeros((1024, 48), w.dtype)
    small[:, 0:16], small[:, 32:48] = dt, a1
    return (np.concatenate([parts[name] for name, _, _ in PHASES]),
            np.ascontiguousarray(small.reshape(8, 128, 48).transpose(1, 0, 2).reshape(128, 384)))


def params(i):
    import numpy as np
    out = np.zeros((128, NPAR), np.float32)

    def put(name, a):
        a = np.asarray(a).reshape(-1, a.shape[-1])
        for t, row in enumerate(a):
            n = row.size // 128
            out[:, PC[name] + t * n:PC[name] + (t + 1) * n] = row.reshape(n, 128).T

    put("mix", i["norm_mix"]); put("mem", i["norm_mem"]); put("xattn", i["norm_xattn"])
    put("ffn", i["norm_ffn"]); put("fin1", i["norm_final"])
    put("sb", i["norm_mix_2"][0:1]); put("lru", i["norm_mix_2"][1:2])
    put("mlp0", i["norm_mlp_2"][0:1]); put("mlp1", i["norm_mlp_2"][1:2]); put("fin2", i["norm_final_2"])
    put("convw", i["ssd_conv_w"][0, :, 0, :]); put("convb", i["ssd_conv_b"])
    put("dskip", np.repeat(i["ssd_D"][0], 64)); put("ssdn", i["ssd_norm"]); put("glan", i["gla_norm"])
    put("glab", i["gla_b_a"])
    out[:16, PC["dtb"]], out[:16, PC["alog"]] = i["ssd_dt_bias"][0], i["ssd_A_log"][0]
    put("lconvw", i["lru_conv_w_2"][0]); put("lconvb", i["lru_conv_b_2"])
    put("brg", i["lru_b_rg_2"]); put("big", i["lru_b_ig_2"]); put("lam", i["lru_lambda_2"])
    return out


def kernel(**inputs):
    import numpy as np
    import concourse.bacc as bacc
    from concourse.bass_utils import run_bass_kernel_spmd

    i = {name: np.asarray(a) for name, a in inputs.items()}

    def tokens(a):
        return np.ascontiguousarray(a.T.reshape(8, 128, -1).transpose(1, 0, 2))

    w, small = stream(i)
    arrays = {
        "w": w, "wsmall": small, "wa2": np.ascontiguousarray(i["gla_w_a2"][0]), "par": params(i),
        "xT": tokens(i["x"][0]), "memT": tokens(i["mem"][0]), "metaT": tokens(i["meta_tokens_2"]),
    }
    nc = bacc.Bacc("TRN2", target_bir_lowering=False, num_devices=1)
    ins = {n: nc.dram_tensor(n, a.shape, mybir.dt.from_np(a.dtype), kind="ExternalInput").ap()
           for n, a in arrays.items()}
    out = nc.dram_tensor("out", (128, 8, 256), F32, kind="ExternalOutput").ap()
    blocks_kernel(nc, out=out, **ins)
    got = run_bass_kernel_spmd(nc, [arrays], core_ids=[0]).results[0]["out"]
    return got.transpose(1, 0, 2).reshape(1024, 256).T.reshape(1, 256, 1024)
```
